# Optimizing a Trainium2 kernel written in Bass

```python
import jax, jax.numpy as jnp
from jax import lax
import numpy as np

D_MODEL = 1024
BATCH = 1
SEQ = 1024
DEPTH = 1

CONV_CH = D_MODEL
CONV_WIDTH = 31
HEAD_DIM = 128
HEADS_PER_GROUP = 4
ATTN_GROUPS = ((128, 1), (512, 4), (2048, 16))
N_GROUPS = len(ATTN_GROUPS)
N_ATTN_HEADS = HEADS_PER_GROUP * N_GROUPS
ATTN_WIDTH = N_ATTN_HEADS * HEAD_DIM
ATTN_OUT_WIDTH = HEADS_PER_GROUP * HEAD_DIM
BLOCK = 128
D_FF = 2816
EPS = 1e-6
IN_WIDTH = 2 * CONV_CH + 3 * ATTN_WIDTH + 2 * D_MODEL

kernel_name = "hybrid_conformer_dilated_attn_block"

def _alibi_slopes():
    h = np.arange(1, N_ATTN_HEADS + 1, dtype=np.float32)
    return np.power(np.float32(2.0), -8.0 * h / np.float32(N_ATTN_HEADS)).astype(np.float32)

def rmsnorm(x, g):
    xf = x.astype(jnp.float32)
    y = xf * lax.rsqrt(jnp.mean(xf * xf, axis=-1, keepdims=True) + EPS)
    return (y * g.astype(jnp.float32)).astype(x.dtype)

def swiglu_ffn(h, w_gate, w_up, w_down):
    return (jax.nn.silu(h @ w_gate) * (h @ w_up)) @ w_down

def conformer_conv(u, dw_kernel, dw_bias, ln_gain, ln_bias, w_out):
    a, b = jnp.split(u, 2, axis=-1)
    z = a * jax.nn.sigmoid(b)
    z = lax.conv_general_dilated(
        z, dw_kernel[:, None, :], window_strides=(1,),
        padding=[(CONV_WIDTH - 1, 0)],
        dimension_numbers=('NWC', 'WIO', 'NWC'),
        feature_group_count=CONV_CH) + dw_bias
    zf = z.astype(jnp.float32)
    mu = jnp.mean(zf, axis=-1, keepdims=True)
    var = jnp.mean(jnp.square(zf - mu), axis=-1, keepdims=True)
    zf = (zf - mu) * lax.rsqrt(var + EPS) * ln_gain.astype(jnp.float32) + ln_bias.astype(jnp.float32)
    z = jax.nn.silu(zf).astype(u.dtype)
    return z @ w_out

def dilated_group_attention(q, k, v, slopes, window, dilation):
    B, S, H, E = q.shape
    span = window // dilation
    chunk = dilation * BLOCK
    s_pad = -(-S // chunk) * chunk
    L = s_pad // dilation
    nb = L // BLOCK

    def to_blocks(t):
        t = jnp.pad(t, ((0, 0), (0, s_pad - S), (0, 0), (0, 0)))
        t = t.reshape(B, L, dilation, H, E)
        t = t.transpose(0, 3, 2, 1, 4)
        return t.reshape(B, H, dilation, nb, BLOCK, E)

    def with_prev(t):
        prev = jnp.pad(t[:, :, :, :-1], ((0, 0), (0, 0), (0, 0), (1, 0), (0, 0), (0, 0)))
        return jnp.concatenate([prev, t], axis=4)

    qb = to_blocks(q)
    kc = with_prev(to_blocks(k))
    vc = with_prev(to_blocks(v))

    scores = jnp.einsum('bhrnqe,bhrnke->bhrnqk', qb, kc).astype(jnp.float32) * (E ** -0.5)
    qi = jnp.arange(BLOCK)[:, None]
    ki = jnp.arange(2 * BLOCK)[None, :]
    steps = BLOCK + qi - ki
    in_band = (steps >= 0) & (steps <= span)
    first_block = (jnp.arange(nb) == 0)[:, None, None]
    valid = in_band[None] & ~(first_block & (ki < BLOCK)[None])
    bias = -slopes[:, None, None] * (dilation * steps).astype(jnp.float32)
    scores = scores + bias[None, :, None, None]
    scores = jnp.where(valid[None, None, None], scores, -jnp.inf)
    m = jnp.max(scores, axis=-1, keepdims=True)
    p = jnp.exp(scores - m)
    denom = jnp.sum(p, axis=-1, keepdims=True)
    out = jnp.einsum('bhrnqk,bhrnke->bhrnqe', p.astype(vc.dtype), vc).astype(jnp.float32) / denom
    lse = (m + jnp.log(denom))[..., 0]

    out = out.astype(q.dtype).reshape(B, H, dilation, L, E).transpose(0, 3, 2, 1, 4)
    out = out.reshape(B, s_pad, H, E)[:, :S]
    lse = lse.reshape(B, H, dilation, L).transpose(0, 3, 2, 1).reshape(B, s_pad, H)[:, :S]
    return out, lse

def setup_inputs(seed: int = 0) -> dict:
    key = jax.random.key(seed)
    ks = jax.random.split(key, 24)

    def w(k, shape, fan_in):
        return jax.random.normal(k, shape, jnp.float32) * (fan_in ** -0.5)

    def gain(k, shape):
        return 1.0 + 0.02 * jax.random.normal(k, shape, jnp.float32)

    def small(k, shape):
        return 0.02 * jax.random.normal(k, shape, jnp.float32)

    Lr = DEPTH
    return {
        "x": jax.random.normal(ks[0], (BATCH, SEQ, D_MODEL), jnp.float32),
        "ffn1_norm": gain(ks[1], (Lr, D_MODEL)),
        "ffn1_w_gate": w(ks[2], (Lr, D_MODEL, D_FF), D_MODEL),
        "ffn1_w_up": w(ks[3], (Lr, D_MODEL, D_FF), D_MODEL),
        "ffn1_w_down": w(ks[4], (Lr, D_FF, D_MODEL), D_FF),
        "mix_norm": gain(ks[5], (Lr, D_MODEL)),
        "w_in": w(ks[6], (Lr, D_MODEL, IN_WIDTH), D_MODEL),
        "conv_dw_kernel": w(ks[7], (Lr, CONV_WIDTH, CONV_CH), CONV_WIDTH),
        "conv_dw_bias": small(ks[8], (Lr, CONV_CH)),
        "conv_ln_gain": gain(ks[9], (Lr, CONV_CH)),
        "conv_ln_bias": small(ks[10], (Lr, CONV_CH)),
        "conv_w_out": w(ks[11], (Lr, CONV_CH, D_MODEL), CONV_CH),
        "attn_w_out": w(ks[12], (Lr, ATTN_OUT_WIDTH, D_MODEL), ATTN_OUT_WIDTH),
        "w_o": w(ks[13], (Lr, D_MODEL, D_MODEL), D_MODEL),
        "ffn2_norm": gain(ks[14], (Lr, D_MODEL)),
        "ffn2_w_gate": w(ks[15], (Lr, D_MODEL, D_FF), D_MODEL),
        "ffn2_w_up": w(ks[16], (Lr, D_MODEL, D_FF), D_MODEL),
        "ffn2_w_down": w(ks[17], (Lr, D_FF, D_MODEL), D_FF),
        "final_norm": gain(ks[18], (D_MODEL,)),
    }

def reference(x, ffn1_norm, ffn1_w_gate, ffn1_w_up, ffn1_w_down, mix_norm, w_in,
              conv_dw_kernel, conv_dw_bias, conv_ln_gain, conv_ln_bias, conv_w_out,
              attn_w_out, w_o, ffn2_norm, ffn2_w_gate, ffn2_w_up, ffn2_w_down, final_norm):
    B, S, _ = x.shape
    slopes = jnp.asarray(_alibi_slopes())
    split_at = [2 * CONV_CH,
                2 * CONV_CH + ATTN_WIDTH,
                2 * CONV_CH + 2 * ATTN_WIDTH,
                2 * CONV_CH + 3 * ATTN_WIDTH,
                2 * CONV_CH + 3 * ATTN_WIDTH + D_MODEL]
    for l in range(DEPTH):
        x = x + 0.5 * swiglu_ffn(rmsnorm(x, ffn1_norm[l]), ffn1_w_gate[l], ffn1_w_up[l], ffn1_w_down[l])

        h = rmsnorm(x, mix_norm[l])
        proj = h @ w_in[l]
        u_conv, q, k, v, g_conv, g_attn = jnp.split(proj, split_at, axis=-1)

        y_conv = conformer_conv(u_conv, conv_dw_kernel[l], conv_dw_bias[l],
                                conv_ln_gain[l], conv_ln_bias[l], conv_w_out[l])

        q = q.reshape(B, S, N_GROUPS, HEADS_PER_GROUP, HEAD_DIM)
        k = k.reshape(B, S, N_GROUPS, HEADS_PER_GROUP, HEAD_DIM)
        v = v.reshape(B, S, N_GROUPS, HEADS_PER_GROUP, HEAD_DIM)
        outs, lses = [], []
        for gi, (window, dilation) in enumerate(ATTN_GROUPS):
            o_g, lse_g = dilated_group_attention(
                q[:, :, gi], k[:, :, gi], v[:, :, gi],
                slopes[gi * HEADS_PER_GROUP:(gi + 1) * HEADS_PER_GROUP], window, dilation)
            outs.append(o_g)
            lses.append(lse_g)
        outs = jnp.stack(outs, axis=0)
        lam = jax.nn.softmax(jnp.stack(lses, axis=0), axis=0)
        attn = jnp.sum(lam[..., None].astype(outs.dtype) * outs, axis=0)
        y_attn = attn.reshape(B, S, ATTN_OUT_WIDTH) @ attn_w_out[l]

        mixed = jax.nn.sigmoid(g_conv) * y_conv + jax.nn.sigmoid(g_attn) * y_attn
        x = x + mixed @ w_o[l]

        x = x + 0.5 * swiglu_ffn(rmsnorm(x, ffn2_norm[l]), ffn2_w_gate[l], ffn2_w_up[l], ffn2_w_down[l])
    return rmsnorm(x, final_norm)


_drawn_inputs = setup_inputs


def setup_inputs(seed=0):
    import zlib

    import numpy as np

    out = dict(_drawn_inputs(seed))
    spreads = {}
    factors = {'ffn1_norm': 6.014,
     'mix_norm': 6.257,
     'conv_dw_bias': 34.26,
     'conv_ln_gain': 172.755,
     'conv_ln_bias': 177.68,
     'ffn2_norm': 28.902,
     'final_norm': 24.284}
    for name, (base, spread) in spreads.items():
        noise = np.random.default_rng([zlib.crc32(name.encode()), seed]).standard_normal(out[name].shape)
        drawn = base * np.exp(spread * noise) if base else spread * noise
        out[name] = __import__('jax').numpy.asarray(drawn.astype(out[name].dtype))
    for name, factor in factors.items():
        out[name] = (out[name] * factor).astype(out[name].dtype)
    return out
```

```python
from contextlib import ExitStack

import numpy as np
import concourse.bass as bass
from concourse import mybir

F32 = mybir.dt.float32
F32R = mybir.dt.float32r
ALU = mybir.AluOpType
ACT = mybir.ActivationFunctionType
AXX = mybir.AxisListType.X

P = 128
SEQ = 1024
D_MODEL = 1024
KT = D_MODEL // P
HALF = 512
D_FF = 2816
CHUNKS = D_FF // (2 * P)
TAPS = 31
PAD = TAPS - 1
ZROW = PAD + SEQ
SLOTS = 4
GROUPS = 3
DILATION = (1, 4, 16)
SCALE = float(P) ** -0.5
EPS = 1e-6
MASKED = 1e30
NBLK = SEQ // P
PAIRS = NBLK // 2

FFN_SLABS = 6 * CHUNKS
A_SLABS = 2 * KT
B_UNITS = 22
SLAB_A = FFN_SLABS
SLAB_B = SLAB_A + A_SLABS
SLAB_C = SLAB_B + 2 * B_UNITS
SLAB_D = SLAB_C + KT
SLAB_E = SLAB_D + 4
SLAB_F = SLAB_E + KT
SLAB_G = SLAB_F + KT
N_SLABS = SLAB_G + FFN_SLABS

V_NORM1, V_MIX, V_NORM2, V_FINAL, V_LNG, V_LNB, V_DWB = range(0, 56, 8)
V_TAPS = 56
N_VEC = V_TAPS + KT * TAPS
C_IDENT, C_MEAN = 0, P
N_CONST = 2 * P
M_SLOPE, M_SEL = 0, 16
N_MIXC = M_SEL + SLOTS * P
N_DIST = 512 + 256


def build_block(nc, w_slabs, x_in, vecs, consts, mix_consts, dists, out):
    x_kept = nc.dram_tensor("x_kept", (KT, P, SEQ), F32, kind="Internal").ap()
    o_kept = nc.dram_tensor("o_kept", (SLOTS, GROUPS, P, SEQ), F32, kind="Internal").ap()
    gates_kept = nc.dram_tensor("gates_kept", (2 * KT, P, SEQ), F32, kind="Internal").ap()

    with ExitStack() as ctx:
        def alloc(name, shape, dt=F32, scope=ctx):
            return scope.enter_context(nc.sbuf_tensor(name, shape, dt))

        def sem(name):
            return ctx.enter_context(nc.semaphore(name))

        raw = alloc("raw", [P, 2, 1024])
        w_hi = [alloc(f"w_hi{i}", [P, 1024], F32R) for i in range(2)]
        w_lo = [alloc(f"w_lo{i}", [P, 1024], F32R) for i in range(2)]
        h_hi = alloc("h_hi", [P, KT, SEQ], F32R)
        h_lo = alloc("h_lo", [P, KT, SEQ], F32R)
        rstd = alloc("rstd", [P, SEQ])
        acc = alloc("acc", [P, SEQ])
        gbuf = alloc("gbuf", [P, 2, HALF])
        hid = alloc("hid", [P, 2, HALF])
        vec = alloc("vec", [P, N_VEC])
        const = alloc("const", [P, N_CONST])
        ident = const[:, C_IDENT:C_IDENT + P]
        mean_ones = const[:, C_MEAN:C_MEAN + P]
        one = alloc("one", [P, 1])
        tok_rstd = alloc("tok_rstd", [P, NBLK])

        with ExitStack() as mixer:
            zbuf = alloc("zbuf", [P, KT + 1, ZROW], scope=mixer)
            mixc = alloc("mixc", [P, N_MIXC], scope=mixer)
            m_stat = alloc("m_stat", [P, SLOTS, GROUPS, NBLK], scope=mixer)
            d_stat = alloc("d_stat", [P, SLOTS, GROUPS, NBLK], scope=mixer)
            with ExitStack() as attention:
                dist = alloc("dist", [P, N_DIST], scope=attention)
                q_t = alloc("q_t", [P, 2, SEQ], scope=attention)
                k_t = alloc("k_t", [P, 2, SEQ], scope=attention)
                v_t = alloc("v_t", [P, SEQ], scope=attention)
                v_tok = alloc("v_tok", [P, NBLK, P], scope=attention)
                o_t = alloc("o_t", [P, SEQ], scope=attention)
                s_buf = alloc("s_buf", [P, 2, 512], scope=attention)
                p_t = alloc("p_t", [P, 2, 512], scope=attention)
                neg_max = alloc("neg_max", [P, 2, 2], scope=attention)
            with ExitStack() as merging:
                a_hi = alloc("a_hi", [P, SLOTS, SEQ], F32R, scope=merging)
                a_lo = alloc("a_lo", [P, SLOTS, SEQ], F32R, scope=merging)
                m_rows = alloc("m_rows", [P, GROUPS, SEQ], scope=merging)
                d_rows = alloc("d_rows", [P, GROUPS, SEQ], scope=merging)
        x_t = alloc("x_t", [P, KT, SEQ])
        with ExitStack() as ffn:
            f_hi = alloc("f_hi", [P, 2, SEQ], F32R, scope=ffn)
            f_lo = alloc("f_lo", [P, 2, SEQ], F32R, scope=ffn)
        with ExitStack() as mixed:
            alloc("gap", [P, KT * (ZROW - SEQ) + 16], scope=mixed)
            mx_hi = alloc("mx_hi", [P, KT, SEQ], F32R, scope=mixed)
            mx_lo = alloc("mx_lo", [P, KT, SEQ], F32R, scope=mixed)
        dist_full = dist[:, 0:512]
        dist_diag = dist[:, 512:768].rearrange("p (a k) -> p a k", a=2)
        o_back = d_rows[:, :, :].rearrange("p g (r t) -> p r g t", r=2)

        ps = ctx.enter_context(nc.psum_tensor("ps", [P, 8, HALF], F32))

        def bank(b):
            return ps[:, b, :]

        slab_loaded = [sem(f"slab_loaded{i}") for i in range(2)]
        slab_rounded, slab_split, slab_used = sem("slab_rounded"), sem("slab_split"), sem("slab_used")
        one_made = sem("one_made")
        vec_loaded, const_loaded, mixc_loaded, dist_loaded = (
            sem("vec_loaded"), sem("const_loaded"), sem("mixc_loaded"), sem("dist_loaded"))
        x_loaded = [[sem(f"x_loaded{d}_{h}") for h in range(2)] for d in range(KT)]
        x_back = [sem(f"x_back{d}") for d in range(KT)]
        x_stored = sem("x_stored")
        gate_ready, gate_scaled, gate_act, gate_weighted = (
            sem("gate_ready"), sem("gate_scaled"), sem("gate_act"), sem("gate_weighted"))
        up_ready, gated, f_rounded, f_ready = (
            sem("up_ready"), sem("gated"), sem("f_rounded"), sem("f_ready"))
        down_ready, down_added = sem("down_ready"), sem("down_added")
        prep_scaled, prep_rounded, prep_ready = sem("prep_scaled"), sem("prep_rounded"), sem("prep_ready")
        squared, square_added = sem("squared"), sem("square_added")
        mean_ready, mean_shifted, root_ready, rstd_ready = (
            sem("mean_ready"), sem("mean_shifted"), sem("root_ready"), sem("rstd_ready"))
        conv_step, ysum_added = sem("conv_step"), sem("ysum_added")
        proj_ready, proj_used = sem("proj_ready"), sem("proj_used")
        side_act = sem("side_act")
        side_stored = [sem(f"side_stored{h}") for h in range(2)]
        scores_ready, s_made, max_made, max_negated = (
            sem("scores_ready"), sem("s_made"), sem("max_made"), sem("max_negated"))
        p_ready, pt_turned, pt_ready = sem("p_ready"), sem("pt_turned"), sem("pt_ready")
        o_ready, o_saved, o_stored = sem("o_ready"), sem("o_saved"), sem("o_stored")
        v_turned, v_ready = sem("v_turned"), sem("v_ready")
        rows_turned, rows_ready, row_step, weights_ready = (
            sem("rows_turned"), sem("rows_ready"), sem("row_step"), sem("weights_ready"))
        exp_ready = sem("exp_ready")
        ymean_ready, centred, ysquared, ysquare_added = (
            sem("ymean_ready"), sem("centred"), sem("ysquared"), sem("ysquare_added"))
        factor_ready, factor_used, merge_step = sem("factor_ready"), sem("factor_used"), sem("merge_step")
        o_back_loaded = [sem(f"o_back_loaded{i}") for i in range(2)]
        merged, a_rounded, a_ready = sem("merged"), sem("a_rounded"), sem("a_ready")
        norm_made, norm_act, norm_rounded, norm_ready = (
            sem("norm_made"), sem("norm_act"), sem("norm_rounded"), sem("norm_ready"))
        gate_back = [sem(f"gate_back{i}") for i in range(2)]
        ya_ready, ya_used = sem("ya_ready"), sem("ya_used")
        yc_ready, yc_gated, mixed_made, mx_rounded, mx_ready = (
            sem("yc_ready"), sem("yc_gated"), sem("mixed_made"), sem("mx_rounded"), sem("mx_ready"))
        wo_ready, wo_added = sem("wo_ready"), sem("wo_added")
        final_made, out_stored = sem("final_made"), sem("out_stored")
        rstd_spread = sem("rstd_spread")

        def tokens(h):
            return slice(h * HALF, (h + 1) * HALF)

        def down_tile(i):
            return 4 * (i // 8) + i % 4, i // 4 % 2

        def tile_major(i):
            return i // 2, i % 2

        def half_major(i):
            return i % KT, i // KT

        def split_natural(ap, dil, h):
            return ap.rearrange("p (i r) -> p r i", r=dil) if dil > 1 else ap

        def split_permuted(ap, dil, h):
            if dil == 1:
                return ap[:, tokens(h)]
            n = HALF // dil
            return ap.rearrange("p (r i) -> p r i", r=dil)[:, :, h * n:(h + 1) * n]

        def pair_in_natural(ap, dil, j):
            if dil == 1:
                return ap[:, 2 * P * j:2 * P * (j + 1)]
            n = 2 * P * dil // SEQ
            v = ap.rearrange("p (i r) -> p r i", r=dil)
            return v[:, n * j:n * (j + 1), :]

        def pair_psum(ap, dil):
            n = 2 * P * dil // SEQ
            return ap.rearrange("p (r i) -> p r i", r=n) if dil > 1 else ap

        def has_prev(g, b):
            return (b > 0, b % 2 == 1, False)[g]

        def pair_span(g, j, x):
            if g == 2:
                return x.rearrange("p (a k) -> p a k", a=2)[:, :, P:2 * P]
            return x if has_prev(g, 2 * j) else x[:, P:512]

        block = ctx.enter_context(nc.Block())

        @block.sync
        def _(sp):
            for i in range(2):
                sp.dma_start(raw[:, i], w_slabs[i]).then_inc(slab_loaded[i], 16)
            with sp.Fori(1, N_SLABS // 2) as it:
                for i in range(2):
                    sp.wait_ge(slab_split, it * 2 + (i - 1))
                    sp.dma_start(raw[:, i], w_slabs[it * 2 + i]).then_inc(slab_loaded[i], 16)
            for i in range(16):
                d, h = half_major(i)
                sp.wait_ge(final_made, i + 1)
                sp.dma_start(out[d][:, tokens(h)], x_t[:, d, tokens(h)]).then_inc(out_stored, 16)
            sp.wait_ge(out_stored, 16 * 16)

        @block.gpsimd
        def _(pool):
            nc.gpsimd.memset(one[:, :], 1.0).then_inc(one_made, 1)
            pool.wait_ge(one_made, 1)

            def split(it, i):
                pool.wait_ge(slab_loaded[i], it * 16 + 16)
                nc.gpsimd.tensor_tensor(w_hi[i][:, :], raw[:, i], one[:, :].to_broadcast([P, 1024]), ALU.mult).then_inc(slab_rounded, 1)
                pool.wait_ge(slab_rounded, it * 2 + (i + 1))
                nc.gpsimd.tensor_tensor(w_lo[i][:, :], raw[:, i], w_hi[i][:, :].bitcast(F32),
                                        ALU.subtract).then_inc(slab_split, 1)

            for i in range(2):
                split(0, i)
            with pool.Fori(1, N_SLABS // 2) as it:
                for i in range(2):
                    pool.wait_ge(slab_used, it * 2 + i)
                    split(it, i)

        @block.tensor
        def _(pe):
            def products(dst, slot, cols, moving, done, opens_slab=False, before=None):
                last = len(cols) - 1
                for k, (c, (m_hi, m_lo)) in enumerate(zip(cols, moving)):
                    if before is not None:
                        before(k)
                    first = pe.matmul(dst, w_hi[slot][:, c], m_hi, start=(k == 0), stop=False)
                    if opens_slab and k == 0:
                        first.then_inc(slab_used, 1)
                    pe.matmul(dst, w_hi[slot][:, c], m_lo, start=False, stop=False)
                    end = pe.matmul(dst, w_lo[slot][:, c], m_hi, start=False, stop=(k == last))
                end.then_inc(done, 1)

            def model_products(dst, slot, h, done, a=h_hi, b=h_lo, before=None):
                products(dst, slot, [slice(k * P, (k + 1) * P) for k in range(KT)],
                         [(a[:, k, tokens(h)], b[:, k, tokens(h)]) for k in range(KT)],
                         done, opens_slab=(h == 0), before=before)

            def tiles_made(made, n, where, h):
                count = {where(i): n + i + 1 for i in range(16)}
                return lambda k: pe.wait_ge(made, count[k, h])

            def statistics(n, src_ready, banks=(6, 7), done=mean_ready):
                pe.wait_ge(const_loaded, 16)
                pe.wait_ge(src_ready, n)
                for h in range(2):
                    pe.matmul(bank(banks[h]), mean_ones, acc[:, tokens(h)],
                              start=True, stop=True).then_inc(done, 1)

            def gated_chunk(c, slab, free, after_two=None, making=None):
                for f in range(2):
                    for w, done in enumerate((gate_ready, up_ready)):
                        for h in range(2):
                            if h == 0:
                                pe.wait_ge(slab_split, slab + (2 * f + w + 1))
                            free(4 * f + 2 * w + h)
                            model_products(bank(4 * f + 2 * w + h), w, h, done,
                                           before=making(h) if making and f + w == 0 else None)
                    if f == 0 and after_two is not None:
                        after_two()

            def ffn_chunk(c, cd, slab, free, after_two=None, making=None):
                gated_chunk(c, slab, free, after_two, making)
                for i in range(16):
                    d, h = down_tile(i)
                    if i % 8 == 0:
                        pe.wait_ge(slab_split, slab + (5 + i // 8))
                    if i % 4 == 0 and i < 8:
                        pe.wait_ge(f_ready, cd * 4 + (3 + h))
                    if i < 8:
                        pe.wait_ge(gate_scaled if i % 4 < 2 else gated, c * 4 + (2 * (i // 4) + i % 2 + 1))
                    else:
                        pe.wait_ge(down_added, cd * 16 + (i - 7))
                    products(bank(i % 8), i // 8,
                             [slice(k * HALF + (d % 4) * P, k * HALF + (d % 4 + 1) * P) for k in range(2)],
                             [(f_hi[:, k, tokens(h)], f_lo[:, k, tokens(h)]) for k in range(2)],
                             down_ready, opens_slab=(i % 8 == 0))

            def first_free(sem_before, count, b, n):
                if b >= 6:
                    pe.wait_ge(mean_shifted, 2 * n + b - 5)
                elif sem_before is not None:
                    pe.wait_ge(sem_before, count + b)

            ffn_chunk(0, 0, 0, lambda b: first_free(None, 0, b, 0), lambda: statistics(16, square_added),
                      lambda h: tiles_made(prep_ready, 0, half_major, h))
            with pe.Fori(1, CHUNKS) as c:
                ffn_chunk(c, c, c * 6, lambda b: pe.wait_ge(down_added, c * 16 + (b - 7)))

            def first_statistics(sem_before, count, n):
                pe.wait_ge(sem_before, count)
                statistics(n, square_added)

            gated_chunk(CHUNKS, SLAB_A, lambda b: first_free(down_added, CHUNKS * 16 - 7, b, 1),
                        lambda: first_statistics(down_added, CHUNKS * 16, 32),
                        lambda h: tiles_made(prep_ready, 16, down_tile, h))
            with pe.Fori(1, 4) as j:
                gated_chunk(None, j * 4 + SLAB_A,
                            lambda b: pe.wait_ge(gate_scaled if b % 4 < 2 else gated,
                                                 j * 4 + (4 * (CHUNKS - 1) + 2 * (b // 4) + b % 2 + 1)))

            def proj_half(b, u, h):
                hu = 2 * u + h
                if h == 0:
                    pe.wait_ge(slab_split, b * B_UNITS + (SLAB_B + u + 1))
                if hu > 3:
                    pe.wait_ge(proj_used, b * 44 + (hu - 3))
                else:
                    pe.wait_ge(gate_scaled if hu < 2 else gated, 4 * (CHUNKS + 3) + hu % 2 + 1)
                if hu == 3:
                    pe.wait_ge(proj_used, b * 43 + 1)
                model_products(bank(hu % 4), u % 2, h, proj_ready)

            def attend(b, m, p):
                g = m % GROUPS
                a4, a2 = b * 24 + 4 * m, b * 12 + 2 * m
                if p >= 2:
                    j = p - 2
                    pe.wait_ge(pt_ready, a4 + (j + 1))
                    pe.wait_ge(v_ready, a2 + 2)
                    if 4 * m + j:
                        pe.wait_ge(o_saved, a4 + j)
                    for q in range(2):
                        parts = [0, 1] if has_prev(g, 2 * j + q) else [1]
                        for part in parts:
                            last = pe.matmul(ps[:, 6, q * P:(q + 1) * P], v_tok[:, 2 * j + q - 1 + part, :],
                                             p_t[:, j % 2, (2 * q + part) * P:(2 * q + part + 1) * P],
                                             start=(part == parts[0]), stop=(part == 1))
                    last.then_inc(o_ready, 1)
                if 1 <= p <= PAIRS:
                    j = p - 1
                    pe.wait_ge(p_ready, a4 + (j + 1))
                    if 4 * m + j:
                        pe.wait_ge(pt_ready, a4 + j)
                    for q in range(2):
                        for part in ([0, 1] if has_prev(g, 2 * j + q) else [1]):
                            at = slice((2 * q + part) * P, (2 * q + part + 1) * P)
                            last = pe.transpose(ps[:, 5, at], s_buf[:, j % 2, at], ident)
                    last.then_inc(pt_turned, 1)
                if p < PAIRS:
                    pe.wait_ge(proj_used, b * 44 + (6 * m + 4))
                    if 4 * m + p:
                        pe.wait_ge(s_made, a4 + p)
                    for q in range(2):
                        blk = 2 * p + q
                        lo = 0 if has_prev(g, blk) else P
                        last = pe.matmul(ps[:, 4, q * 256 + lo:(q + 1) * 256],
                                         q_t[:, m % 2, blk * P:(blk + 1) * P],
                                         k_t[:, m % 2, blk * P - P + lo:(blk + 1) * P],
                                         start=True, stop=True)
                    last.then_inc(scores_ready, 1)
                if p < 2:
                    pe.wait_ge(proj_used, b * 44 + (6 * m + 6))
                    if 2 * m + p:
                        pe.wait_ge(v_ready, a2 + p)
                    for i in range(4):
                        blk = 4 * p + i
                        last = pe.transpose(ps[:, 7, i * P:(i + 1) * P], v_t[:, blk * P:(blk + 1) * P], ident)
                    last.then_inc(v_turned, 1)

            with pe.Fori(0, 2) as b:
                for hu in range(2 * B_UNITS):
                    proj_half(b, hu // 2, hu % 2)
                    if hu == 6:
                        pe.wait_ge(gate_scaled, 4 * (CHUNKS + 4))
                        pe.wait_ge(gated, 4 * (CHUNKS + 4))
                    if 6 <= hu < 42:
                        attend(b, hu // 6 - 1, hu % 6)
                pe.wait_ge(proj_used, b * 44 + 43)

            def stat_rows(i):
                src = (m_stat, d_stat)[i // 3]
                if i > 0:
                    pe.wait_ge(rows_ready, i)
                for blk in range(NBLK):
                    last = pe.transpose(ps[0:SLOTS, 6 + blk // 4, (blk % 4) * P:(blk % 4 + 1) * P],
                                        src[:, :, i % 3, blk], ident)
                last.then_inc(rows_turned, 1)

            def factors(n):
                s, h = tile_major(n)
                for g in range(GROUPS):
                    i = GROUPS * n + g
                    if i >= 4:
                        pe.wait_ge(factor_used, i - 3)
                    pe.matmul(bank(4 + i % 4), mixc[0:SLOTS, M_SEL + s * P:M_SEL + (s + 1) * P],
                              m_rows[0:SLOTS, g, tokens(h)], start=True, stop=True).then_inc(factor_ready, 1)

            for hu in range(2 * KT):
                if hu % 2 == 0:
                    pe.wait_ge(slab_split, SLAB_C + hu // 2 + 1)
                pe.wait_ge(proj_used, 88 + hu - 3)
                model_products(bank(hu % 4), hu // 2 % 2, hu % 2, proj_ready)
                if hu == 0:
                    pe.wait_ge(o_saved, 48)
                    statistics(KT + 1, ysum_added, (4, 5), ymean_ready)
                if 1 <= hu <= 6:
                    stat_rows(hu - 1)
                if hu == 8:
                    pe.wait_ge(rows_ready, 6)
                    statistics(16, ysquare_added)
                if hu == 12:
                    pe.wait_ge(weights_ready, 3)
                    pe.wait_ge(mean_shifted, 6)
                if hu >= 12:
                    factors(hu - 12)
            for n in range(4, 8):
                factors(n)

            for i in range(16):
                d, h = tile_major(i)
                if i % 4 == 0:
                    pe.wait_ge(slab_split, SLAB_D + i // 4 + 1)
                if i < 2:
                    pe.wait_ge(a_ready, 7 + i)
                if i < 4:
                    pe.wait_ge(proj_used, 101 + i)
                elif i < 8:
                    pe.wait_ge(factor_used, 24)
                else:
                    pe.wait_ge(ya_used, i - 7)
                products(bank(i % 8), i // 4 % 2,
                         [slice(k * 256 + (d % 2) * P, k * 256 + (d % 2 + 1) * P) for k in range(SLOTS)],
                         [(a_hi[:, k, tokens(h)], a_lo[:, k, tokens(h)]) for k in range(SLOTS)],
                         ya_ready, opens_slab=(i % 4 == 0))

            for i in range(16):
                if i % 2 == 0:
                    pe.wait_ge(slab_split, SLAB_E + i // 2 + 1)
                if i < 8:
                    pe.wait_ge(ya_used, i + 9)
                else:
                    pe.wait_ge(yc_gated, i - 7)
                model_products(bank(i % 8), i // 2 % 2, i % 2, yc_ready,
                               before=tiles_made(norm_ready, 0, tile_major, i) if i < 2 else None)

            for i in range(16):
                if i % 2 == 0:
                    pe.wait_ge(slab_split, SLAB_F + i // 2 + 1)
                if i < 8:
                    pe.wait_ge(yc_gated, i + 9)
                else:
                    pe.wait_ge(wo_added, i - 7)
                model_products(bank(i % 8), i // 2 % 2, i % 2, wo_ready, mx_hi, mx_lo,
                               before=tiles_made(mx_ready, 0, tile_major, i) if i < 2 else None)

            ffn_chunk(CHUNKS + 4, CHUNKS, SLAB_G, lambda b: first_free(wo_added, 9, b, 3),
                      lambda: first_statistics(wo_added, 16, 48),
                      lambda h: tiles_made(prep_ready, 32, tile_major, h))
            with pe.Fori(CHUNKS + 1, 2 * CHUNKS) as c:
                ffn_chunk(c + 4, c, c * 6 + (SLAB_G - 6 * CHUNKS),
                          lambda b: pe.wait_ge(down_added, c * 16 + (b - 7)))
            pe.wait_ge(down_added, 32 * CHUNKS)
            pe.wait_ge(square_added, 64)
            for blk in range(NBLK):
                last = pe.matmul(ps[:, 6, blk:blk + 1], acc[:, blk * P:(blk + 1) * P], mean_ones[:, 0:1],
                                 start=True, stop=True)
            last.then_inc(mean_ready, 1)
            pe.wait_ge(rstd_ready, 9)
            for blk in range(NBLK):
                last = pe.matmul(ps[:, blk // 4, (blk % 4) * P:(blk % 4 + 1) * P],
                                 tok_rstd[:, blk:blk + 1].to_broadcast([P, P]), ident, start=True, stop=True)
                if blk % 4 == 3:
                    last.then_inc(rstd_spread, 1)

        @block.scalar
        def _(act):
            act.dma_start(vec[:, :], vecs).then_inc(vec_loaded, 16)
            for i in range(16):
                d, h = half_major(i)
                act.dma_start(x_t[:, d, tokens(h)], x_in[d][:, tokens(h)]).then_inc(x_loaded[d][h], 16)
            act.dma_start(const[:, :], consts).then_inc(const_loaded, 16)

            def prep(n, where, squares=False):
                for i in range(16):
                    d, h = where(i)
                    act.wait_ge(prep_scaled, 16 * n + i + 1)
                    nc.scalar.activation(h_hi[:, d, tokens(h)], hid[:, i % 2], ACT.Copy).then_inc(prep_rounded, 1)
                    if n == 1 and h == 1:
                        act.dma_start(x_kept[d], x_t[:, d]).then_inc(x_stored, 16)
                    if squares:
                        square(n, i, where)

            def square(n, i, where):
                d, h = where(i)
                if i >= 2:
                    act.wait_ge(square_added, 16 * n + i - 1)
                nc.scalar.activation(gbuf[:, i % 2], x_t[:, d, tokens(h)], ACT.Square).then_inc(squared, 1)

            def squares(n, where):
                for i in range(16):
                    square(n, i, where)

            def root(n, dst=rstd):
                for h in range(2):
                    act.wait_ge(mean_shifted, 2 * n + h + 1)
                    nc.scalar.activation(dst[:, tokens(h)], dst[:, tokens(h)], ACT.Sqrt).then_inc(root_ready, 1)

            def gate(c, f, func):
                for h in range(2):
                    act.wait_ge(gate_scaled, c * 4 + (2 * f + h + 1))
                    nc.scalar.activation(gbuf[:, h], gbuf[:, h], func).then_inc(gate_act, 1)

            def ffn_chunk(c):
                for f in range(2):
                    gate(c, f, ACT.Silu)
                    for h in range(2):
                        act.wait_ge(gated, c * 4 + (2 * f + h + 1))
                        nc.scalar.activation(f_hi[:, f, tokens(h)], hid[:, h], ACT.Copy).then_inc(f_rounded, 1)

            prep(0, half_major)
            squares(0, half_major)
            root(0)
            ffn_chunk(0)
            with act.Fori(1, CHUNKS) as c:
                ffn_chunk(c)
            prep(1, down_tile)
            squares(1, down_tile)
            root(1)

            act.wait_ge(x_stored, 16 * KT)
            act.dma_start(mixc[:, :], mix_consts).then_inc(mixc_loaded, 16)
            act.dma_start(dist[:, :], dists).then_inc(dist_loaded, 16)
            with act.Fori(CHUNKS, CHUNKS + 4) as c:
                for f in range(2):
                    gate(c, f, ACT.Sigmoid)

            def side_gate(n, tile, h):
                nc.scalar.activation(gbuf[:, h], gbuf[:, h], ACT.Sigmoid).then_inc(side_act, 1)
                act.wait_ge(side_act, n)
                act.dma_start(gates_kept[tile][:, tokens(h)], gbuf[:, h]).then_inc(side_stored[h], 16)

            def attend(b, m, p):
                g = m % GROUPS
                a4, a2, slot = b * 24 + 4 * m, b * 12 + 2 * m, b * 2 + m // GROUPS
                if p >= 2:
                    j = p - 2
                    act.wait_ge(o_ready, a4 + (j + 1))
                    if j == 0 and m > 0:
                        act.wait_ge(o_stored, b * 96 + 16 * m)
                    nc.scalar.activation(pair_in_natural(o_t[:, :], DILATION[g], j),
                                         pair_psum(ps[:, 6, 0:2 * P], DILATION[g]), ACT.Copy).then_inc(o_saved, 1)
                    if j == PAIRS - 1:
                        act.wait_ge(o_saved, a4 + PAIRS)
                        act.dma_start(o_kept[slot, g], o_t[:, :]).then_inc(o_stored, 16)
                if 1 <= p <= PAIRS:
                    j = p - 1
                    act.wait_ge(pt_turned, a4 + (j + 1))
                    nc.scalar.activation(pair_span(g, j, p_t[:, j % 2, :]), pair_span(g, j, ps[:, 5, :]),
                                         ACT.Copy).then_inc(pt_ready, 1)
                if p < 2:
                    act.wait_ge(v_turned, a2 + (p + 1))
                    nc.scalar.activation(v_tok[:, 4 * p:4 * p + 4, :],
                                         ps[:, 7, :].rearrange("p (b e) -> p b e", b=4), ACT.Copy).then_inc(v_ready, 1)
                if p < PAIRS:
                    act.wait_ge(max_negated, a4 + (p + 1))
                    for q in range(2):
                        blk = 2 * p + q
                        at = slice(q * 256 + (0 if has_prev(g, blk) else P), (q + 1) * 256)
                        last = nc.scalar.activation(s_buf[:, p % 2, at], s_buf[:, p % 2, at], ACT.Exp,
                                                    bias=neg_max[:, p % 2, q:q + 1], scale=SCALE,
                                                    accum_out=d_stat[:, slot, g, blk:blk + 1])
                    last.then_inc(p_ready, 1)

            with act.Fori(0, 2) as b:
                for hu in range(6, 2 * B_UNITS):
                    if hu >= 36:
                        i = hu - 36
                        act.wait_ge(proj_used, b * 44 + (hu + 1))
                        side_gate(b * 8 + (i + 1), b * 4 + i // 2, i % 2)
                    if hu < 42:
                        attend(b, hu // 6 - 1, hu % 6)
                act.wait_ge(o_stored, b * 96 + 96)

            def side(i):
                act.wait_ge(proj_used, 89 + i)
                side_gate(17 + i, KT + i // 2, i % 2)

            def rows(i):
                dst, dil = (m_rows, d_rows)[i // 3][0:SLOTS, i % 3, :], DILATION[i % 3]
                act.wait_ge(rows_turned, i + 1)
                for h in range(2):
                    src = ps[0:SLOTS, 6 + h, :]
                    if dil == 1:
                        view = dst[:, tokens(h)]
                    else:
                        view = dst.rearrange("p (i r) -> p r i", r=dil)[:, h * dil // 2:(h + 1) * dil // 2, :]
                        src = src.rearrange("p (r i) -> p r i", r=dil // 2)
                    last = nc.scalar.activation(view, src, ACT.Copy)
                last.then_inc(rows_ready, 1)

            def ysquare(d):
                for h in range(2):
                    i = 2 * d + h
                    act.wait_ge(centred, i + 1)
                    if i >= 2:
                        act.wait_ge(ysquare_added, i - 1)
                    nc.scalar.activation(hid[:, h], zbuf[:, d, tokens(h)], ACT.Square).then_inc(ysquared, 1)

            def merge(n):
                s, h = tile_major(n)
                act.wait_ge(merged, n + 1)
                nc.scalar.activation(a_hi[:, s, tokens(h)], o_back[:, n % 2, 0], ACT.Copy).then_inc(a_rounded, 1)

            def load_o(n):
                s, h = tile_major(n)
                if n >= 2:
                    act.wait_ge(a_ready, n - 1)
                act.dma_start(o_back[:, n % 2], o_kept[s].rearrange("g e t -> e g t")[:, :, tokens(h)])\
                   .then_inc(o_back_loaded[n % 2], 16)

            side(0)
            side(1)
            for k in range(4):
                ysquare(2 * k)
                ysquare(2 * k + 1)
                rows(k)
                side(k + 2)
            rows(4)
            side(6)
            rows(5)
            for g in range(GROUPS):
                act.wait_ge(row_step, 3 + g)
                nc.scalar.activation(m_rows[0:SLOTS, g, :], m_rows[0:SLOTS, g, :], ACT.Exp,
                                     scale=SCALE).then_inc(exp_ready, 1)
            for i in range(7, 11):
                side(i)
            act.wait_ge(weights_ready, 3)
            act.wait_ge(o_stored, 16 * SLOTS * GROUPS)
            load_o(0)
            load_o(1)
            for h in range(2):
                act.wait_ge(mean_shifted, 4 + h + 1)
                nc.scalar.activation(acc[:, tokens(h)], acc[:, tokens(h)], ACT.Sqrt).then_inc(root_ready, 1)
            side(11)
            side(12)
            for n in range(8):
                merge(n)
                if n < 3:
                    side(13 + n)
                if n + 2 < 8:
                    load_o(n + 2)

            def load_gate(n):
                if n >= 2:
                    act.wait_ge(ya_used if n < 18 else yc_gated, n - 1 if n < 18 else n - 17)
                tile, h = tile_major(n)
                act.dma_start(gbuf[:, n % 2], gates_kept[(tile + KT) % (2 * KT)][:, tokens(h)])\
                   .then_inc(gate_back[n % 2], 16)

            for h in range(2):
                act.wait_ge(side_stored[h], 16 * 16)
            load_gate(0)
            load_gate(1)
            for i in range(16):
                d, h = tile_major(i)
                act.wait_ge(norm_made, i + 1)
                nc.scalar.activation(hid[:, i % 2], hid[:, i % 2], ACT.Silu,
                                     bias=vec[:, V_LNB + d:V_LNB + d + 1]).then_inc(norm_act, 1)
                act.wait_ge(norm_act, i + 1)
                nc.scalar.activation(h_hi[:, d, tokens(h)], hid[:, i % 2], ACT.Copy).then_inc(norm_rounded, 1)
                if i >= 1:
                    load_gate(i + 1)
            load_gate(17)

            for i in range(16):
                d, h = tile_major(i)
                act.wait_ge(mixed_made, i + 1)
                nc.scalar.activation(mx_hi[:, d, tokens(h)], hid[:, i % 2], ACT.Copy).then_inc(mx_rounded, 1)
                if i + 2 < 16:
                    load_gate(18 + i)

            act.wait_ge(mixed_made, 16)
            for d in range(KT):
                act.dma_start(x_t[:, d], x_kept[d]).then_inc(x_back[d], 16)
            prep(2, tile_major, squares=True)
            root(3)

            ffn_chunk(CHUNKS + 4)
            with act.Fori(CHUNKS + 5, 2 * CHUNKS + 4) as c:
                ffn_chunk(c)
            for i in range(16):
                act.wait_ge(down_added, 16 * (2 * CHUNKS - 1) + i + 1)
                square(3, i, down_tile)
            act.wait_ge(mean_shifted, 9)
            nc.scalar.activation(tok_rstd[:, :], tok_rstd[:, :], ACT.Sqrt).then_inc(root_ready, 1)

        @block.vector
        def _(dve):
            v = nc.vector

            def prep_scale(n, i, gain, where):
                d, h = where(i)
                if i >= 2:
                    dve.wait_ge(prep_ready, 16 * n + i - 1)
                v.tensor_scalar(hid[:, i % 2], x_t[:, d, tokens(h)], vec[:, gain + d:gain + d + 1], None,
                                ALU.mult).then_inc(prep_scaled, 1)

            def prep_rest(n, i, where):
                d, h = where(i)
                dve.wait_ge(prep_rounded, 16 * n + i + 1)
                v.tensor_tensor(h_lo[:, d, tokens(h)], hid[:, i % 2], h_hi[:, d, tokens(h)].bitcast(F32),
                                ALU.subtract).then_inc(prep_ready, 1)

            def add_square(n, i, where):
                d, h = where(i)
                dve.wait_ge(squared, 16 * n + i + 1)
                if d == 0:
                    v.tensor_copy(acc[:, tokens(h)], gbuf[:, i % 2]).then_inc(square_added, 1)
                else:
                    before = max(k for k in range(i) if where(k)[1] == h)
                    dve.wait_ge(square_added, 16 * n + before + 1)
                    v.tensor_tensor(acc[:, tokens(h)], acc[:, tokens(h)], gbuf[:, i % 2],
                                    ALU.add).then_inc(square_added, 1)

            def inverse_root(n, m, dst=rstd):
                for h in range(2):
                    dve.wait_ge(mean_ready, 2 * n + h + 1)
                    v.tensor_scalar(dst[:, tokens(h)], bank(6 + h), EPS, None, ALU.add).then_inc(mean_shifted, 1)
                for h in range(2):
                    dve.wait_ge(root_ready, m + h + 1)
                    v.reciprocal(dst[:, tokens(h)], dst[:, tokens(h)]).then_inc(rstd_ready, 1)
                dve.wait_ge(rstd_ready, 2 * n + 2)

            def gate(c, f, first=False):
                for h in range(2):
                    dve.wait_ge(gate_ready, c * 4 + (2 * f + h + 1))
                    if f == 1 or not first:
                        dve.wait_ge(gated, c * 4 + (2 * f + h - 1))
                    v.tensor_tensor(gbuf[:, h], bank(4 * f + h), rstd[:, tokens(h)], ALU.mult)\
                     .then_inc(gate_scaled, 1)
                    dve.wait_ge(gate_act, c * 4 + (2 * f + h + 1))
                    v.tensor_tensor(gbuf[:, h], gbuf[:, h], rstd[:, tokens(h)], ALU.mult)\
                     .then_inc(gate_weighted, 1)

            def up(c, f, h, dst):
                dve.wait_ge(up_ready, c * 4 + (2 * f + h + 1))
                dve.wait_ge(gate_weighted, c * 4 + (2 * f + h + 1))
                v.tensor_tensor(dst, bank(4 * f + 2 + h), gbuf[:, h], ALU.mult).then_inc(gated, 1)

            def ffn_gates(c, cf, first=False):
                for f in range(2):
                    gate(c, f, first)
                    for h in range(2):
                        if f == 1:
                            dve.wait_ge(f_ready, cf * 4 + (h + 1))
                        up(c, f, h, hid[:, h])
                        dve.wait_ge(f_rounded, cf * 4 + (2 * f + h + 1))
                        v.tensor_tensor(f_lo[:, f, tokens(h)], hid[:, h], f_hi[:, f, tokens(h)].bitcast(F32),
                                        ALU.subtract).then_inc(f_ready, 1)

            def add_down(cd, i):
                d, h = down_tile(i)
                dve.wait_ge(down_ready, cd * 16 + (i + 1))
                v.scalar_tensor_tensor(x_t[:, d, tokens(h)], bank(i % 8), 0.5, x_t[:, d, tokens(h)],
                                       ALU.mult, ALU.add).then_inc(down_added, 1)

            dve.wait_ge(vec_loaded, 16)
            for i in range(17):
                if i < 16:
                    d, h = half_major(i)
                    dve.wait_ge(x_loaded[d][h], 16)
                    prep_scale(0, i, V_NORM1, half_major)
                if i >= 1:
                    prep_rest(0, i - 1, half_major)
            for i in range(16):
                add_square(0, i, half_major)
            inverse_root(0, 0)
            ffn_gates(0, 0, first=True)
            for i in range(16):
                add_down(0, i)
            with dve.Fori(1, CHUNKS - 1) as c:
                ffn_gates(c, c)
                for i in range(16):
                    add_down(c, i)
            ffn_gates(CHUNKS - 1, CHUNKS - 1)
            for i in range(17):
                if i < 16:
                    add_down(CHUNKS - 1, i)
                    dve.wait_ge(down_added, 16 * (CHUNKS - 1) + i + 1)
                    prep_scale(1, i, V_MIX, down_tile)
                if i >= 1:
                    prep_rest(1, i - 1, down_tile)
            for i in range(16):
                add_square(1, i, down_tile)
            inverse_root(1, 2)

            dve.wait_ge(x_stored, 16 * KT)
            v.memset(zbuf[:, :, 0:PAD], 0.0).then_inc(conv_step, 1)
            v.memset(acc[:, :], 0.0).then_inc(ysum_added, 1)

            def conv_taps(tile, first, end):
                y = zbuf[:, tile, 0:SEQ]
                for t in range(first, end):
                    z = zbuf[:, tile + 1, t:t + SEQ]
                    k = vec[:, bass.ds(tile * TAPS + (V_TAPS + t), 1)]
                    if t == 0:
                        dve.wait_ge(conv_step, tile * TAPS + 1)
                        v.tensor_scalar(y, z, k, vec[:, bass.ds(tile + V_DWB, 1)], ALU.mult, ALU.add)\
                         .then_inc(conv_step, 1)
                    else:
                        dve.wait_ge(conv_step, tile * TAPS + (t + 1))
                        v.scalar_tensor_tensor(y, z, k, y, ALU.mult, ALU.add).then_inc(conv_step, 1)
                if end == TAPS:
                    dve.wait_ge(conv_step, tile * TAPS + (TAPS + 1))
                    dve.wait_ge(ysum_added, tile + 1)
                    v.tensor_tensor(acc[:, :], acc[:, :], y, ALU.add).then_inc(ysum_added, 1)

            with dve.Fori(0, 2) as j:
                for q in range(4):
                    c = j * 2 + (CHUNKS + q // 2)
                    if q == 1:
                        dve.wait_ge(gated, j * 2 + (4 * CHUNKS + 2))
                    gate(c, q % 2)
                    if q > 0:
                        conv_taps(j, TAPS * (q - 1) // 3, TAPS * (2 * q - 1) // 6)
                    for h in range(2):
                        up(c, q % 2, h, zbuf[:, j * 4 + (q + 1), PAD + h * HALF:PAD + (h + 1) * HALF])
                        if q > 0 and h == 0:
                            conv_taps(j, TAPS * (2 * q - 1) // 6, TAPS * q // 3)

            def take_proj(b, u, h):
                m, kind = u // 3, u % 3
                dil = DILATION[m % GROUPS]
                dst = (q_t[:, m % 2, :], k_t[:, m % 2, :], v_t[:, :])[kind]
                dve.wait_ge(proj_ready, b * 44 + (2 * u + h + 1))
                v.tensor_tensor(split_permuted(dst, dil, h), split_natural(bank((2 * u + h) % 4), dil, h),
                                split_natural(rstd[:, tokens(h)], dil, h), ALU.mult).then_inc(proj_used, 1)

            def take_gate(b, u, h, n):
                dve.wait_ge(proj_ready, b * 44 + (2 * u + h + 1))
                if n is not None:
                    dve.wait_ge(side_stored[h], n)
                v.tensor_tensor(gbuf[:, h], bank((2 * u + h) % 4), rstd[:, tokens(h)], ALU.mult)\
                 .then_inc(proj_used, 1)

            def soften(b, m, p):
                g = m % GROUPS
                a4, slot = b * 24 + 4 * m, b * 2 + m // GROUPS
                dst = s_buf[:, p % 2, :]
                d = dist_diag if g == 2 else (dist_full if has_prev(g, 2 * p) else dist_full[:, P:512])
                dve.wait_ge(scores_ready, a4 + (p + 1))
                v.scalar_tensor_tensor(pair_span(g, p, dst), d, mixc[:, bass.ds(slot * GROUPS + (M_SLOPE + g), 1)],
                                       pair_span(g, p, ps[:, 4, :]), ALU.mult, ALU.add).then_inc(s_made, 1)
                dve.wait_ge(s_made, a4 + (p + 1))
                peaks = m_stat[:, slot, g, 2 * p:2 * p + 2]
                if g == 2 or has_prev(g, 2 * p):
                    s = dst.rearrange("p (a k) -> p a k", a=2)
                    v.tensor_reduce(peaks, s[:, :, P:256] if g == 2 else s, AXX, ALU.max).then_inc(max_made, 2)
                else:
                    v.tensor_reduce(peaks[:, 0:1], dst[:, P:256], AXX, ALU.max).then_inc(max_made, 1)
                    v.tensor_reduce(peaks[:, 1:2], dst[:, 256:512], AXX, ALU.max).then_inc(max_made, 1)
                dve.wait_ge(max_made, a4 * 2 + (2 * p + 2))
                v.tensor_scalar(neg_max[:, p % 2, :], peaks, -SCALE, None, ALU.mult).then_inc(max_negated, 1)

            dve.wait_ge(mixc_loaded, 16)
            dve.wait_ge(dist_loaded, 16)
            with dve.Fori(0, 2) as b:
                for hu in range(2 * B_UNITS):
                    u, h = tile_major(hu)
                    if u < 18:
                        take_proj(b, u, h)
                    else:
                        take_gate(b, u, h, b * 64 + 16 * (u - 18) if u > 18 else None)
                    if 6 <= hu < 42 and hu % 6 < PAIRS:
                        soften(b, hu // 6 - 1, hu % 6)
                    if hu == 0:
                        dve.wait_ge(gated, 4 * (CHUNKS + 4))
                    i = hu % 14
                    if hu < 42:
                        conv_taps(b * 3 + (2 + hu // 14), TAPS * i // 14, TAPS * (i + 1) // 14)
                for h in range(2):
                    dve.wait_ge(side_stored[h], b * 64 + 64)

            def side(i):
                take_gate(2, i // 2, i % 2, 128 + 16 * (i // 2))

            def centre(d):
                for h in range(2):
                    dve.wait_ge(ymean_ready, h + 1)
                    v.tensor_tensor(zbuf[:, d, tokens(h)], zbuf[:, d, tokens(h)], bank(4 + h),
                                    ALU.subtract).then_inc(centred, 1)
                for h in range(2):
                    i = 2 * d + h
                    dve.wait_ge(ysquared, i + 1)
                    if d == 0:
                        v.tensor_copy(acc[:, tokens(h)], hid[:, h]).then_inc(ysquare_added, 1)
                    else:
                        dve.wait_ge(ysquare_added, i - 1)
                        v.tensor_tensor(acc[:, tokens(h)], acc[:, tokens(h)], hid[:, h],
                                        ALU.add).then_inc(ysquare_added, 1)

            dve.wait_ge(ysum_added, KT + 1)
            side(0)
            side(1)
            for k in range(4):
                centre(2 * k)
                centre(2 * k + 1)
                side(k + 2)
            side(6)
            top = hid[0:SLOTS, :, :].rearrange("p a t -> p (a t)")
            m_g = [m_rows[0:SLOTS, g, :] for g in range(GROUPS)]
            d_g = [d_rows[0:SLOTS, g, :] for g in range(GROUPS)]
            dve.wait_ge(rows_ready, 6)
            dve.wait_ge(ysquare_added, 16)
            v.tensor_tensor(top, m_g[0], m_g[1], ALU.max).then_inc(row_step, 1)
            dve.wait_ge(row_step, 1)
            v.tensor_tensor(top, top, m_g[2], ALU.max).then_inc(row_step, 1)
            dve.wait_ge(row_step, 2)
            for g in range(GROUPS):
                v.tensor_tensor(m_g[g], m_g[g], top, ALU.subtract).then_inc(row_step, 1)
            side(7)
            for g in range(GROUPS):
                dve.wait_ge(exp_ready, g + 1)
                v.tensor_tensor(d_g[g], d_g[g], m_g[g], ALU.mult).then_inc(row_step, 1)
            side(8)
            dve.wait_ge(row_step, 7)
            v.tensor_tensor(d_g[0], d_g[0], d_g[1], ALU.add).then_inc(row_step, 1)
            dve.wait_ge(row_step, 9)
            v.tensor_tensor(d_g[0], d_g[0], d_g[2], ALU.add).then_inc(row_step, 1)
            dve.wait_ge(row_step, 10)
            v.reciprocal(d_g[0], d_g[0]).then_inc(row_step, 1)
            side(9)
            dve.wait_ge(row_step, 11)
            for g in range(GROUPS):
                v.tensor_tensor(m_g[g], m_g[g], d_g[0], ALU.mult).then_inc(weights_ready, 1)
            side(10)
            for h in range(2):
                dve.wait_ge(mean_ready, 4 + h + 1)
                v.tensor_scalar(acc[:, tokens(h)], bank(6 + h), EPS, None, ALU.add).then_inc(mean_shifted, 1)
            side(11)
            for h in range(2):
                dve.wait_ge(root_ready, 4 + h + 1)
                v.reciprocal(acc[:, tokens(h)], acc[:, tokens(h)]).then_inc(rstd_ready, 1)
            side(12)

            def merge(n):
                s, h = tile_major(n)
                o = [o_back[:, n % 2, g] for g in range(GROUPS)]
                dve.wait_ge(o_back_loaded[n % 2], 16 * (n // 2 + 1))
                for g in range(GROUPS):
                    i = GROUPS * n + g
                    dve.wait_ge(factor_ready, i + 1)
                    v.tensor_tensor(o[g], o[g], bank(4 + i % 4), ALU.mult).then_inc(factor_used, 1)
                dve.wait_ge(factor_used, GROUPS * n + 2)
                v.tensor_tensor(o[0], o[0], o[1], ALU.add).then_inc(merge_step, 1)
                dve.wait_ge(merge_step, n + 1)
                dve.wait_ge(factor_used, GROUPS * n + 3)
                v.tensor_tensor(o[0], o[0], o[2], ALU.add).then_inc(merged, 1)
                dve.wait_ge(a_rounded, n + 1)
                v.tensor_tensor(a_lo[:, s, tokens(h)], o[0], a_hi[:, s, tokens(h)].bitcast(F32),
                                ALU.subtract).then_inc(a_ready, 1)

            for n in range(8):
                merge(n)
                if n < 3:
                    side(13 + n)

            dve.wait_ge(rstd_ready, 6)
            for i in range(17):
                if i < 16:
                    d, h = tile_major(i)
                    if i >= 2:
                        dve.wait_ge(norm_ready, i - 1)
                    v.scalar_tensor_tensor(hid[:, i % 2], zbuf[:, d, tokens(h)], vec[:, V_LNG + d:V_LNG + d + 1],
                                           acc[:, tokens(h)], ALU.mult, ALU.mult).then_inc(norm_made, 1)
                if i >= 1:
                    d, h = tile_major(i - 1)
                    dve.wait_ge(norm_rounded, i)
                    v.tensor_tensor(h_lo[:, d, tokens(h)], hid[:, (i - 1) % 2], h_hi[:, d, tokens(h)].bitcast(F32),
                                    ALU.subtract).then_inc(norm_ready, 1)
                    dve.wait_ge(ya_ready, i)
                    dve.wait_ge(gate_back[(i - 1) % 2], 16 * ((i - 1) // 2 + 1))
                    v.tensor_tensor(zbuf[:, d, tokens(h)], bank((i - 1) % 8), gbuf[:, (i - 1) % 2],
                                    ALU.mult).then_inc(ya_used, 1)

            for i in range(17):
                if i < 16:
                    d, h = tile_major(i)
                    dve.wait_ge(yc_ready, i + 1)
                    dve.wait_ge(gate_back[i % 2], 16 * (8 + i // 2 + 1))
                    dve.wait_ge(mx_ready if i >= 2 else norm_ready, i - 1 if i >= 2 else 16)
                    v.tensor_tensor(hid[:, i % 2], bank(i % 8), gbuf[:, i % 2], ALU.mult).then_inc(yc_gated, 1)
                    dve.wait_ge(yc_gated, i + 1)
                    dve.wait_ge(ya_used, i + 1)
                    v.tensor_tensor(hid[:, i % 2], hid[:, i % 2], zbuf[:, d, tokens(h)], ALU.add)\
                     .then_inc(mixed_made, 1)
                if i >= 1:
                    d, h = tile_major(i - 1)
                    dve.wait_ge(mx_rounded, i)
                    v.tensor_tensor(mx_lo[:, d, tokens(h)], hid[:, (i - 1) % 2], mx_hi[:, d, tokens(h)].bitcast(F32),
                                    ALU.subtract).then_inc(mx_ready, 1)

            for i in range(17):
                if i < 16:
                    d, h = tile_major(i)
                    dve.wait_ge(wo_ready, i + 1)
                    dve.wait_ge(x_back[d], 16)
                    v.tensor_tensor(x_t[:, d, tokens(h)], bank(i % 8), x_t[:, d, tokens(h)], ALU.add)\
                     .then_inc(wo_added, 1)
                    dve.wait_ge(wo_added, i + 1)
                    prep_scale(2, i, V_NORM2, tile_major)
                if i >= 1:
                    prep_rest(2, i - 1, tile_major)
                    add_square(2, i - 1, tile_major)
            inverse_root(3, 6)

            ffn_gates(CHUNKS + 4, CHUNKS)
            for i in range(16):
                add_down(CHUNKS, i)
            with dve.Fori(CHUNKS + 1, 2 * CHUNKS - 1) as c:
                ffn_gates(c + 4, c)
                for i in range(16):
                    add_down(c, i)
            ffn_gates(2 * CHUNKS + 3, 2 * CHUNKS - 1)
            for i in range(17):
                if i < 16:
                    add_down(2 * CHUNKS - 1, i)
                if i >= 1:
                    add_square(3, i - 1, down_tile)
            dve.wait_ge(mean_ready, 9)
            v.tensor_scalar(tok_rstd[:, :], ps[:, 6, 0:NBLK], EPS, None, ALU.add).then_inc(mean_shifted, 1)
            dve.wait_ge(root_ready, 9)
            v.reciprocal(tok_rstd[:, :], tok_rstd[:, :]).then_inc(rstd_ready, 1)
            for i in range(16):
                d, h = half_major(i)
                dve.wait_ge(rstd_spread, h + 1)
                v.scalar_tensor_tensor(x_t[:, d, tokens(h)], x_t[:, d, tokens(h)], vec[:, V_FINAL + d:V_FINAL + d + 1],
                                       bank(h), ALU.mult, ALU.mult).then_inc(final_made, 1)


def _shape_constants():
    consts = np.zeros((P, N_CONST), np.float32)
    consts[:, C_IDENT:C_IDENT + P] = np.eye(P)
    consts[:, C_MEAN:C_MEAN + P] = 1.0 / D_MODEL
    mixc = np.zeros((P, N_MIXC), np.float32)
    heads = np.arange(1, SLOTS * GROUPS + 1, dtype=np.float32)
    slopes = np.power(np.float32(2.0), -8.0 * heads / np.float32(SLOTS * GROUPS))
    for s in range(SLOTS):
        for g in range(GROUPS):
            mixc[:, M_SLOPE + s * GROUPS + g] = -slopes[g * SLOTS + s] * DILATION[g] / SCALE
        mixc[s, M_SEL + s * P:M_SEL + (s + 1) * P] = 1.0
    q, k = np.arange(P)[:, None], np.arange(2 * P)[None, :]
    steps = P + q - k
    full = np.where((steps >= 0) & (steps <= P), steps, MASKED)
    k = np.arange(P)[None, :]
    own = P // 2
    diag = np.where((q // own == k // own) & (q >= k), q - k, MASKED)
    dists = np.concatenate([full, full, diag, diag], axis=1).astype(np.float32)
    return consts, mixc, dists


def _columns(w, first):
    return w[:, first:first + P].reshape(KT, P, P).transpose(1, 0, 2).reshape(P, 1024)


def _ffn_slabs(gate, up, down):
    for c in range(CHUNKS):
        for f in range(2):
            yield _columns(gate, (2 * c + f) * P)
            yield _columns(up, (2 * c + f) * P)
        rows = down[2 * c * P:2 * (c + 1) * P].reshape(2, P, 2, HALF)
        for j in range(2):
            yield rows[:, :, j].transpose(1, 0, 2).reshape(P, 1024)


def _slabs(t):
    w_in = t["w_in"][0]
    q0 = 2 * D_MODEL
    width = SLOTS * GROUPS * P
    gates0 = q0 + 3 * width
    yield from _ffn_slabs(t["ffn1_w_gate"][0], t["ffn1_w_up"][0], t["ffn1_w_down"][0])
    for i in range(KT):
        yield _columns(w_in, D_MODEL + i * P)
        yield _columns(w_in, i * P)
    for b in range(2):
        for s in (2 * b, 2 * b + 1):
            for g in range(GROUPS):
                for kind in range(3):
                    yield _columns(w_in, q0 + kind * width + (g * SLOTS + s) * P)
        for i in range(4):
            yield _columns(w_in, gates0 + (4 * b + i) * P)
    for i in range(KT):
        yield _columns(w_in, gates0 + D_MODEL + i * P)
    rows = t["attn_w_out"][0].reshape(SLOTS, P, 4, 256)
    for j in range(4):
        yield rows[:, :, j].transpose(1, 0, 2).reshape(P, 1024)
    for i in range(KT):
        yield _columns(t["conv_w_out"][0], i * P)
    for i in range(KT):
        yield _columns(t["w_o"][0], i * P)
    yield from _ffn_slabs(t["ffn2_w_gate"][0], t["ffn2_w_up"][0], t["ffn2_w_down"][0])


def kernel(**inputs):
    import concourse.bacc as _bacc
    from concourse.bass_utils import run_bass_kernel_spmd as _run

    t = {name: np.asarray(a) for name, a in inputs.items()}
    feature_cols = [t[n].reshape(KT, P).T for n in
                    ("ffn1_norm", "mix_norm", "ffn2_norm", "final_norm", "conv_ln_gain", "conv_ln_bias",
                     "conv_dw_bias")]
    taps = t["conv_dw_kernel"][0].reshape(TAPS, KT, P).transpose(2, 1, 0).reshape(P, KT * TAPS)
    consts, mixc, dists = _shape_constants()
    arrays = {
        "w_slabs": np.stack(list(_slabs(t))),
        "x_in": np.ascontiguousarray(t["x"][0].T).reshape(KT, P, SEQ),
        "vecs": np.ascontiguousarray(np.concatenate(feature_cols + [taps], axis=1)),
        "consts": consts,
        "mix_consts": mixc,
        "dists": dists,
    }
    nc = _bacc.Bacc("TRN2", target_bir_lowering=False, num_devices=1)
    args = [nc.dram_tensor(n, a.shape, F32, kind="ExternalInput").ap() for n, a in arrays.items()]
    out = nc.dram_tensor("out_t", (KT, P, SEQ), F32, kind="ExternalOutput").ap()
    build_block(nc, *args, out)
    r = _run(nc, [arrays], core_ids=[0])
    return np.ascontiguousarray(r.results[0]["out_t"].reshape(1, D_MODEL, SEQ).transpose(0, 2, 1))
```

```python
from contextlib import ExitStack

import numpy as np
import concourse.bass as bass
from concourse import mybir

F32 = mybir.dt.float32
F32R = mybir.dt.float32r
ALU = mybir.AluOpType
ACT = mybir.ActivationFunctionType
AXX = mybir.AxisListType.X

P = 128
SEQ = 1024
D_MODEL = 1024
KT = D_MODEL // P
HALF = 512
D_FF = 2816
CHUNKS = D_FF // (2 * P)
TAPS = 31
PAD = TAPS - 1
ZROW = PAD + SEQ
SLOTS = 4
GROUPS = 3
DILATION = (1, 4, 16)
SCALE = float(P) ** -0.5
EPS = 1e-6
MASKED = 1e30
NBLK = SEQ // P
PAIRS = NBLK // 2

FFN_SLABS = 6 * CHUNKS
A_SLABS = 2 * KT
B_UNITS = 22
SLAB_A = FFN_SLABS
SLAB_B = SLAB_A + A_SLABS
SLAB_C = SLAB_B + 2 * B_UNITS
SLAB_D = SLAB_C + KT
SLAB_E = SLAB_D + 4
SLAB_F = SLAB_E + KT
SLAB_G = SLAB_F + KT
N_SLABS = SLAB_G + FFN_SLABS

V_NORM1, V_MIX, V_NORM2, V_FINAL, V_LNG, V_LNB, V_DWB = range(0, 56, 8)
V_TAPS = 56
N_VEC = V_TAPS + KT * TAPS
C_IDENT, C_MEAN = 0, P
N_CONST = 2 * P
N_SLOPES = SLOTS * GROUPS
N_DIST = 512 + 256


def build_block(nc, w_slabs, x_in, vecs, consts, slopes_in, dists, out):
    x_kept = nc.dram_tensor("x_kept", (KT, P, SEQ), F32, kind="Internal").ap()
    o_kept = nc.dram_tensor("o_kept", (SLOTS, GROUPS, P, SEQ), F32, kind="Internal").ap()
    factors_kept = nc.dram_tensor("factors_kept", (SLOTS, GROUPS, SEQ), F32, kind="Internal").ap()
    gates_kept = nc.dram_tensor("gates_kept", (2 * KT, P, SEQ), F32, kind="Internal").ap()

    with ExitStack() as ctx:
        def alloc(name, shape, dt=F32, scope=ctx):
            return scope.enter_context(nc.sbuf_tensor(name, shape, dt))

        def sem(name):
            return ctx.enter_context(nc.semaphore(name))

        raw = alloc("raw", [P, 2, 1024])
        w_hi = [alloc(f"w_hi{i}", [P, 1024], F32R) for i in range(2)]
        w_lo = [alloc(f"w_lo{i}", [P, 1024], F32R) for i in range(2)]
        h_hi = alloc("h_hi", [P, KT, SEQ], F32R)
        h_lo = alloc("h_lo", [P, KT, SEQ], F32R)
        rstd = alloc("rstd", [P, SEQ])
        acc = alloc("acc", [P, SEQ])
        gbuf = alloc("gbuf", [P, 2, HALF])
        hid = alloc("hid", [P, 2, HALF])
        vec = alloc("vec", [P, N_VEC])
        const = alloc("const", [P, N_CONST])
        ident = const[:, C_IDENT:C_IDENT + P]
        mean_ones = const[:, C_MEAN:C_MEAN + P]
        one = alloc("one", [P, 1])
        tok_rstd = alloc("tok_rstd", [P, NBLK])

        with ExitStack() as mixer:
            zbuf = alloc("zbuf", [P, KT + 1, ZROW], scope=mixer)
            slopes = alloc("slopes", [P, N_SLOPES], scope=mixer)
            m_stat = alloc("m_stat", [P, SLOTS, GROUPS, NBLK], scope=mixer)
            d_stat = alloc("d_stat", [P, SLOTS, GROUPS, NBLK], scope=mixer)
            with ExitStack() as attention:
                dist = alloc("dist", [P, N_DIST], scope=attention)
                q_t = alloc("q_t", [P, 2, SEQ], scope=attention)
                k_t = alloc("k_t", [P, 2, SEQ], scope=attention)
                v_t = alloc("v_t", [P, SEQ], scope=attention)
                v_tok = alloc("v_tok", [P, NBLK, P], scope=attention)
                o_t = alloc("o_t", [P, SEQ], scope=attention)
                s_buf = alloc("s_buf", [P, 2, 512], scope=attention)
                p_t = alloc("p_t", [P, 2, 512], scope=attention)
                neg_max = alloc("neg_max", [P, 2, 2], scope=attention)
            with ExitStack() as ahead:
                o_ahead = []
                for name in ("a_hi", "a_lo"):
                    alloc(f"slots_0_1_of_{name}", [P, 2, SEQ], scope=ahead)
                    o_ahead.append(alloc(f"o_under_{name}", [P, 4, HALF], scope=ahead))
            with ExitStack() as merging:
                a_hi = alloc("a_hi", [P, SLOTS, SEQ], F32R, scope=merging)
                a_lo = alloc("a_lo", [P, SLOTS, SEQ], F32R, scope=merging)
                m_rows = alloc("m_rows", [P, GROUPS, SEQ], scope=merging)
                d_rows = alloc("d_rows", [P, GROUPS, SEQ], scope=merging)
                y_mean = alloc("y_mean", [P, SEQ], scope=merging)
        x_t = alloc("x_t", [P, KT, SEQ])
        with ExitStack() as ffn:
            f_hi = alloc("f_hi", [P, 2, SEQ], F32R, scope=ffn)
            f_lo = alloc("f_lo", [P, 2, SEQ], F32R, scope=ffn)
        with ExitStack() as mixed:
            alloc("gap", [P, KT * (ZROW - SEQ) + 16], scope=mixed)
            mx_hi = alloc("mx_hi", [P, KT, SEQ], F32R, scope=mixed)
            mx_lo = alloc("mx_lo", [P, KT, SEQ], F32R, scope=mixed)
        dist_full = dist[:, 0:512]
        dist_diag = dist[:, 512:768].rearrange("p (a k) -> p a k", a=2)
        o_after = d_rows[:, :, :].rearrange("p g (r t) -> p r g t", r=2)
        factor_back = m_rows[:, :, :].rearrange("p g (r t) -> p r g t", r=2)

        y_square = zbuf[:, KT, 0:SEQ].rearrange("p (h t) -> p h t", h=2)

        ps = ctx.enter_context(nc.psum_tensor("ps", [P, 8, HALF], F32))

        def bank(b):
            return ps[:, b, :]

        projection_banks = (4, 5, 0, 1, 2, 3, 6, 7)

        def projection_bank(i):
            return bank(projection_banks[i % 8])

        slab_loaded = [sem(f"slab_loaded{i}") for i in range(2)]
        slab_rounded, slab_split, slab_used = sem("slab_rounded"), sem("slab_split"), sem("slab_used")
        one_made = sem("one_made")
        vec_loaded, const_loaded, slopes_loaded, dist_loaded = (
            sem("vec_loaded"), sem("const_loaded"), sem("slopes_loaded"), sem("dist_loaded"))
        x_loaded = [[sem(f"x_loaded{d}_{h}") for h in range(2)] for d in range(KT)]
        x_back = [sem(f"x_back{d}") for d in range(KT)]
        x_stored = sem("x_stored")
        gate_ready, gate_scaled, gate_act, gate_weighted = (
            sem("gate_ready"), sem("gate_scaled"), sem("gate_act"), sem("gate_weighted"))
        up_ready, gated, f_rounded, f_ready = (
            sem("up_ready"), sem("gated"), sem("f_rounded"), sem("f_ready"))
        down_ready, down_added = sem("down_ready"), sem("down_added")
        prep_scaled, prep_rounded, prep_ready = sem("prep_scaled"), sem("prep_rounded"), sem("prep_ready")
        squared, square_added = sem("squared"), sem("square_added")
        mean_ready, mean_shifted, root_ready, rstd_ready = (
            sem("mean_ready"), sem("mean_shifted"), sem("root_ready"), sem("rstd_ready"))
        conv_step, ysum_added = sem("conv_step"), sem("ysum_added")
        proj_ready, proj_used = sem("proj_ready"), sem("proj_used")
        side_act = sem("side_act")
        side_stored = [sem(f"side_stored{h}") for h in range(2)]
        scores_ready, s_made, max_made, max_negated = (
            sem("scores_ready"), sem("s_made"), sem("max_made"), sem("max_negated"))
        p_ready, pt_turned, pt_ready = sem("p_ready"), sem("pt_turned"), sem("pt_ready")
        o_ready, o_saved, o_stored = sem("o_ready"), sem("o_saved"), sem("o_stored")
        v_turned, v_ready = sem("v_turned"), sem("v_ready")
        rows_turned, rows_ready, row_step, weights_ready = (
            sem("rows_turned"), sem("rows_ready"), sem("row_step"), sem("weights_ready"))
        exp_ready = sem("exp_ready")
        mean_saved = sem("mean_saved")
        ymean_ready, centred, ysquared, ysquare_added = (
            sem("ymean_ready"), sem("centred"), sem("ysquared"), sem("ysquare_added"))
        factors_stored, factor_used, merge_step = sem("factors_stored"), sem("factor_used"), sem("merge_step")
        factor_loaded = [sem(f"factor_loaded{i}") for i in range(2)]
        o_back_loaded = [sem(f"o_back_loaded{i}") for i in range(4)]
        merged, a_rounded, a_ready = sem("merged"), sem("a_rounded"), sem("a_ready")
        norm_made, norm_act, norm_rounded, norm_ready = (
            sem("norm_made"), sem("norm_act"), sem("norm_rounded"), sem("norm_ready"))
        gate_back = [sem(f"gate_back{i}") for i in range(2)]
        ya_ready, ya_used = sem("ya_ready"), sem("ya_used")
        yc_ready, yc_gated, mixed_made, mx_rounded, mx_ready = (
            sem("yc_ready"), sem("yc_gated"), sem("mixed_made"), sem("mx_rounded"), sem("mx_ready"))
        wo_ready, wo_added = sem("wo_ready"), sem("wo_added")
        final_made, out_stored = sem("final_made"), sem("out_stored")
        rstd_spread = sem("rstd_spread")

        def tokens(h):
            return slice(h * HALF, (h + 1) * HALF)

        def down_tile(i):
            return 4 * (i // 8) + i % 4, i // 4 % 2

        def tile_major(i):
            return i // 2, i % 2

        def o_back(n):
            return o_ahead[n][:, 0:GROUPS] if n < 2 else o_after[:, n % 2]

        def half_major(i):
            return i % KT, i // KT

        def split_natural(ap, dil, h):
            return ap.rearrange("p (i r) -> p r i", r=dil) if dil > 1 else ap

        def split_permuted(ap, dil, h):
            if dil == 1:
                return ap[:, tokens(h)]
            n = HALF // dil
            return ap.rearrange("p (r i) -> p r i", r=dil)[:, :, h * n:(h + 1) * n]

        def pair_in_natural(ap, dil, j):
            if dil == 1:
                return ap[:, 2 * P * j:2 * P * (j + 1)]
            n = 2 * P * dil // SEQ
            v = ap.rearrange("p (i r) -> p r i", r=dil)
            return v[:, n * j:n * (j + 1), :]

        def pair_psum(ap, dil):
            n = 2 * P * dil // SEQ
            return ap.rearrange("p (r i) -> p r i", r=n) if dil > 1 else ap

        def has_prev(g, b):
            return (b > 0, b % 2 == 1, False)[g]

        def pair_span(g, j, x):
            if g == 2:
                return x.rearrange("p (a k) -> p a k", a=2)[:, :, P:2 * P]
            return x if has_prev(g, 2 * j) else x[:, P:512]

        block = ctx.enter_context(nc.Block())

        @block.sync
        def _(sp):
            for i in range(2):
                sp.dma_start(raw[:, i], w_slabs[i]).then_inc(slab_loaded[i], 16)
            for d in range(KT):
                sp.dma_start(x_t[:, d, tokens(1)], x_in[d][:, tokens(1)]).then_inc(x_loaded[d][1], 16)
            sp.dma_start(const[:, :], consts).then_inc(const_loaded, 16)
            with sp.Fori(1, N_SLABS // 2) as it:
                for i in range(2):
                    sp.wait_ge(slab_split, it * 2 + (i - 1))
                    sp.dma_start(raw[:, i], w_slabs[it * 2 + i]).then_inc(slab_loaded[i], 16)
            for i in range(16):
                d, h = half_major(i)
                sp.wait_ge(final_made, i + 1)
                sp.dma_start(out[d][:, tokens(h)], x_t[:, d, tokens(h)]).then_inc(out_stored, 16)
            sp.wait_ge(out_stored, 16 * 16)

        @block.gpsimd
        def _(pool):
            nc.gpsimd.memset(one[:, :], 1.0).then_inc(one_made, 1)
            pool.wait_ge(one_made, 1)

            def split(it, i):
                pool.wait_ge(slab_loaded[i], it * 16 + 16)
                nc.gpsimd.tensor_tensor(w_hi[i][:, :], raw[:, i], one[:, :].to_broadcast([P, 1024]), ALU.mult).then_inc(slab_rounded, 1)
                pool.wait_ge(slab_rounded, it * 2 + (i + 1))
                nc.gpsimd.tensor_tensor(w_lo[i][:, :], raw[:, i], w_hi[i][:, :].bitcast(F32),
                                        ALU.subtract).then_inc(slab_split, 1)

            for i in range(2):
                split(0, i)
            def split_next(it, i):
                pool.wait_ge(slab_used, it * 2 + i)
                split(it, i)

            def centre(i):
                d, h = tile_major(i)
                pool.wait_ge(mean_saved, h + 1)
                nc.gpsimd.tensor_tensor(zbuf[:, d, tokens(h)], zbuf[:, d, tokens(h)], y_mean[:, tokens(h)],
                                        ALU.subtract).then_inc(centred, 1)

            def add_ysquare(i):
                d, h = tile_major(i)
                pool.wait_ge(ysquared, i + 1)
                if d == 0:
                    nc.gpsimd.tensor_copy(acc[:, tokens(h)], y_square[:, h]).then_inc(ysquare_added, 1)
                else:
                    pool.wait_ge(ysquare_added, i - 1)
                    nc.gpsimd.tensor_tensor(acc[:, tokens(h)], acc[:, tokens(h)], y_square[:, h],
                                            ALU.add).then_inc(ysquare_added, 1)

            with pool.Fori(1, SLAB_C // 2) as it:
                for i in range(2):
                    split_next(it, i)
            sums_before = (0, 0, 2, 4, 7, 8, 10, 12, 14, 17, 17)
            for n in range(10):
                split_next(SLAB_C // 2 + n // 2, n % 2)
                for i in range(sums_before[n], sums_before[n + 1]):
                    if i < 16:
                        centre(i)
                    if 1 <= i <= 16:
                        add_ysquare(i - 1)
            with pool.Fori(SLAB_D // 2 + 1, N_SLABS // 2) as it:
                for i in range(2):
                    split_next(it, i)

        @block.tensor
        def _(pe):
            def products(dst, slot, cols, moving, done, opens_slab=False, before=None):
                last = len(cols) - 1
                for k, (c, (m_hi, m_lo)) in enumerate(zip(cols, moving)):
                    if before is not None:
                        before(k)
                    first = pe.matmul(dst, w_hi[slot][:, c], m_hi, start=(k == 0), stop=False)
                    if opens_slab and k == 0:
                        first.then_inc(slab_used, 1)
                    pe.matmul(dst, w_hi[slot][:, c], m_lo, start=False, stop=False)
                    end = pe.matmul(dst, w_lo[slot][:, c], m_hi, start=False, stop=(k == last))
                end.then_inc(done, 1)

            def model_products(dst, slot, h, done, a=h_hi, b=h_lo, before=None):
                products(dst, slot, [slice(k * P, (k + 1) * P) for k in range(KT)],
                         [(a[:, k, tokens(h)], b[:, k, tokens(h)]) for k in range(KT)],
                         done, opens_slab=(h == 0), before=before)

            def tiles_made(made, n, where, h):
                count = {where(i): n + i + 1 for i in range(16)}
                return lambda k: pe.wait_ge(made, count[k, h])

            def statistics(n, src_ready, banks=(6, 7), done=mean_ready):
                pe.wait_ge(const_loaded, 16)
                pe.wait_ge(src_ready, n)
                for h in range(2):
                    pe.matmul(bank(banks[h]), mean_ones, acc[:, tokens(h)],
                              start=True, stop=True).then_inc(done, 1)

            def gated_chunk(c, slab, free, after_two=None, making=None):
                for f in range(2):
                    for w, done in enumerate((gate_ready, up_ready)):
                        for h in range(2):
                            if h == 0:
                                pe.wait_ge(slab_split, slab + (2 * f + w + 1))
                            free(4 * f + 2 * w + h)
                            model_products(bank(4 * f + 2 * w + h), w, h, done,
                                           before=making(h) if making and f + w == 0 else None)
                    if f == 0 and after_two is not None:
                        after_two()

            def ffn_chunk(c, cd, slab, free, after_two=None, making=None):
                gated_chunk(c, slab, free, after_two, making)
                for i in range(16):
                    d, h = down_tile(i)
                    if i % 8 == 0:
                        pe.wait_ge(slab_split, slab + (5 + i // 8))
                    if i % 4 == 0 and i < 8:
                        pe.wait_ge(f_ready, cd * 4 + (3 + h))
                    if i < 8:
                        pe.wait_ge(gate_scaled if i % 4 < 2 else gated, c * 4 + (2 * (i // 4) + i % 2 + 1))
                    else:
                        pe.wait_ge(down_added, cd * 16 + (i - 7))
                    products(bank(i % 8), i // 8,
                             [slice(k * HALF + (d % 4) * P, k * HALF + (d % 4 + 1) * P) for k in range(2)],
                             [(f_hi[:, k, tokens(h)], f_lo[:, k, tokens(h)]) for k in range(2)],
                             down_ready, opens_slab=(i % 8 == 0))

            def first_free(sem_before, count, b, n):
                if b >= 6:
                    pe.wait_ge(mean_shifted, 2 * n + b - 5)
                elif sem_before is not None:
                    pe.wait_ge(sem_before, count + b)

            ffn_chunk(0, 0, 0, lambda b: first_free(None, 0, b, 0), lambda: statistics(16, square_added),
                      lambda h: tiles_made(prep_ready, 0, half_major, h))
            with pe.Fori(1, CHUNKS) as c:
                ffn_chunk(c, c, c * 6, lambda b: pe.wait_ge(down_added, c * 16 + (b - 7)))

            def first_statistics(sem_before, count, n):
                pe.wait_ge(sem_before, count)
                statistics(n, square_added)

            gated_chunk(CHUNKS, SLAB_A, lambda b: first_free(down_added, CHUNKS * 16 - 7, b, 1),
                        lambda: first_statistics(down_added, CHUNKS * 16, 32),
                        lambda h: tiles_made(prep_ready, 16, down_tile, h))
            with pe.Fori(1, 4) as j:
                gated_chunk(None, j * 4 + SLAB_A,
                            lambda b: pe.wait_ge(gate_scaled if b % 4 < 2 else gated,
                                                 j * 4 + (4 * (CHUNKS - 1) + 2 * (b // 4) + b % 2 + 1)))

            def proj_half(b, u, h):
                hu = 2 * u + h
                if h == 0:
                    pe.wait_ge(slab_split, b * B_UNITS + (SLAB_B + u + 1))
                if hu > 3:
                    pe.wait_ge(proj_used, b * 44 + (hu - 3))
                else:
                    pe.wait_ge(gate_scaled if hu < 2 else gated, 4 * (CHUNKS + 3) + hu % 2 + 1)
                if hu == 3:
                    pe.wait_ge(proj_used, b * 43 + 1)
                model_products(bank(hu % 4), u % 2, h, proj_ready)

            def attend(b, m, p):
                g = m % GROUPS
                a4, a2 = b * 24 + 4 * m, b * 12 + 2 * m
                if p >= 2:
                    j = p - 2
                    pe.wait_ge(pt_ready, a4 + (j + 1))
                    pe.wait_ge(v_ready, a2 + 2)
                    if 4 * m + j:
                        pe.wait_ge(o_saved, a4 + j)
                    for q in range(2):
                        parts = [0, 1] if has_prev(g, 2 * j + q) else [1]
                        for part in parts:
                            last = pe.matmul(ps[:, 6, q * P:(q + 1) * P], v_tok[:, 2 * j + q - 1 + part, :],
                                             p_t[:, j % 2, (2 * q + part) * P:(2 * q + part + 1) * P],
                                             start=(part == parts[0]), stop=(part == 1))
                    last.then_inc(o_ready, 1)
                if 1 <= p <= PAIRS:
                    j = p - 1
                    pe.wait_ge(p_ready, a4 + (j + 1))
                    if 4 * m + j:
                        pe.wait_ge(pt_ready, a4 + j)
                    for q in range(2):
                        for part in ([0, 1] if has_prev(g, 2 * j + q) else [1]):
                            at = slice((2 * q + part) * P, (2 * q + part + 1) * P)
                            last = pe.transpose(ps[:, 5, at], s_buf[:, j % 2, at], ident)
                    last.then_inc(pt_turned, 1)
                if p < PAIRS:
                    pe.wait_ge(proj_used, b * 44 + (6 * m + 4))
                    if 4 * m + p:
                        pe.wait_ge(s_made, a4 + p)
                    for q in range(2):
                        blk = 2 * p + q
                        lo = 0 if has_prev(g, blk) else P
                        last = pe.matmul(ps[:, 4, q * 256 + lo:(q + 1) * 256],
                                         q_t[:, m % 2, blk * P:(blk + 1) * P],
                                         k_t[:, m % 2, blk * P - P + lo:(blk + 1) * P],
                                         start=True, stop=True)
                    last.then_inc(scores_ready, 1)
                if p < 2:
                    pe.wait_ge(proj_used, b * 44 + (6 * m + 6))
                    if 2 * m + p:
                        pe.wait_ge(v_ready, a2 + p)
                    for i in range(4):
                        blk = 4 * p + i
                        last = pe.transpose(ps[:, 7, i * P:(i + 1) * P], v_t[:, blk * P:(blk + 1) * P], ident)
                    last.then_inc(v_turned, 1)

            with pe.Fori(0, 2) as b:
                for hu in range(2 * B_UNITS):
                    proj_half(b, hu // 2, hu % 2)
                    if hu == 6:
                        pe.wait_ge(gate_scaled, 4 * (CHUNKS + 4))
                        pe.wait_ge(gated, 4 * (CHUNKS + 4))
                    if 6 <= hu < 42:
                        attend(b, hu // 6 - 1, hu % 6)
                pe.wait_ge(proj_used, b * 44 + 43)

            def stat_rows(i):
                src = (m_stat, d_stat)[i // 3]
                if i == 1:
                    pe.wait_ge(mean_saved, 2)
                if i > 1:
                    pe.wait_ge(rows_ready, i - 1)
                for blk in range(NBLK):
                    last = pe.transpose(ps[0:SLOTS, 4 + i % 2 * 2 + blk // 4, (blk % 4) * P:(blk % 4 + 1) * P],
                                        src[:, :, i % 3, blk], ident)
                last.then_inc(rows_turned, 1)

            for hu in range(2 * KT):
                if hu % 2 == 0:
                    pe.wait_ge(slab_split, SLAB_C + hu // 2 + 1)
                if hu < 4:
                    pe.wait_ge(proj_used, 88 + hu - 3)
                elif hu < 6:
                    pe.wait_ge(rows_ready, 5)
                else:
                    pe.wait_ge(proj_used, 88 + hu - 5)
                model_products(bank(hu % 6), hu // 2 % 2, hu % 2, proj_ready)
                if hu == 0:
                    pe.wait_ge(o_saved, 48)
                    statistics(KT + 1, ysum_added, (6, 7), ymean_ready)
                    stat_rows(0)
                if hu == 1:
                    stat_rows(1)
                    stat_rows(2)
                if hu == 2:
                    stat_rows(3)
                    stat_rows(4)
                    stat_rows(5)

            pe.wait_ge(slab_split, SLAB_D + 1)
            for k in range(SLOTS):
                for i in range(4):
                    d, h = tile_major(i)
                    c = slice(k * 256 + d * P, k * 256 + (d + 1) * P)
                    if k == 0:
                        pe.wait_ge(proj_used, 99 + i)
                    if d == 0:
                        pe.wait_ge(a_ready, 2 * k + h + 1)
                    first = pe.matmul(projection_bank(i), w_hi[0][:, c], a_hi[:, k, tokens(h)], start=(k == 0), stop=False)
                    if k == 0 and i == 0:
                        first.then_inc(slab_used, 1)
                    pe.matmul(projection_bank(i), w_hi[0][:, c], a_lo[:, k, tokens(h)], start=False, stop=False)
                    end = pe.matmul(projection_bank(i), w_lo[0][:, c], a_hi[:, k, tokens(h)],
                                    start=False, stop=(k == SLOTS - 1))
                    if k == SLOTS - 1:
                        end.then_inc(ya_ready, 1)
                if k == 1:
                    pe.wait_ge(rows_ready, 6)
                    statistics(16, ysquare_added)
            for i in range(4, 16):
                d, h = tile_major(i)
                if i % 4 == 0:
                    pe.wait_ge(slab_split, SLAB_D + i // 4 + 1)
                if i < 6:
                    pe.wait_ge(proj_used, 99 + i)
                elif i < 8:
                    pe.wait_ge(mean_shifted, 6)
                else:
                    pe.wait_ge(ya_used, i - 7)
                products(projection_bank(i), i // 4 % 2,
                         [slice(k * 256 + (d % 2) * P, k * 256 + (d % 2 + 1) * P) for k in range(SLOTS)],
                         [(a_hi[:, k, tokens(h)], a_lo[:, k, tokens(h)]) for k in range(SLOTS)],
                         ya_ready, opens_slab=(i % 4 == 0))

            for i in range(16):
                if i % 2 == 0:
                    pe.wait_ge(slab_split, SLAB_E + i // 2 + 1)
                if i < 8:
                    pe.wait_ge(ya_used, i + 9)
                else:
                    pe.wait_ge(yc_gated, i - 7)
                model_products(projection_bank(i), i // 2 % 2, i % 2, yc_ready,
                               before=tiles_made(norm_ready, 0, tile_major, i) if i < 2 else None)

            for i in range(16):
                if i % 2 == 0:
                    pe.wait_ge(slab_split, SLAB_F + i // 2 + 1)
                if i < 8:
                    pe.wait_ge(yc_gated, 9 + projection_banks.index(i))
                else:
                    pe.wait_ge(wo_added, i - 7)
                model_products(bank(i % 8), i // 2 % 2, i % 2, wo_ready, mx_hi, mx_lo,
                               before=tiles_made(mx_ready, 0, tile_major, i) if i < 2 else None)

            ffn_chunk(CHUNKS + 4, CHUNKS, SLAB_G, lambda b: first_free(wo_added, 9, b, 3),
                      lambda: first_statistics(wo_added, 16, 48),
                      lambda h: tiles_made(prep_ready, 32, tile_major, h))
            with pe.Fori(CHUNKS + 1, 2 * CHUNKS) as c:
                ffn_chunk(c + 4, c, c * 6 + (SLAB_G - 6 * CHUNKS),
                          lambda b: pe.wait_ge(down_added, c * 16 + (b - 7)))
            pe.wait_ge(down_added, 32 * CHUNKS)
            pe.wait_ge(square_added, 64)
            for blk in range(NBLK):
                last = pe.matmul(ps[:, 6, blk:blk + 1], acc[:, blk * P:(blk + 1) * P], mean_ones[:, 0:1],
                                 start=True, stop=True)
            last.then_inc(mean_ready, 1)
            pe.wait_ge(rstd_ready, 9)
            for blk in range(NBLK):
                last = pe.matmul(ps[:, blk // 4, (blk % 4) * P:(blk % 4 + 1) * P],
                                 tok_rstd[:, blk:blk + 1].to_broadcast([P, P]), ident, start=True, stop=True)
                if blk % 4 == 3:
                    last.then_inc(rstd_spread, 1)

        @block.scalar
        def _(act):
            act.dma_start(vec[:, :], vecs).then_inc(vec_loaded, 16)
            for d in range(KT):
                act.dma_start(x_t[:, d, tokens(0)], x_in[d][:, tokens(0)]).then_inc(x_loaded[d][0], 16)

            def prep(n, where, squares=False):
                for i in range(16):
                    d, h = where(i)
                    act.wait_ge(prep_scaled, 16 * n + i + 1)
                    nc.scalar.activation(h_hi[:, d, tokens(h)], hid[:, i % 2], ACT.Copy).then_inc(prep_rounded, 1)
                    if n == 1 and h == 1:
                        act.dma_start(x_kept[d], x_t[:, d]).then_inc(x_stored, 16)
                    if squares:
                        square(n, i, where)

            def square(n, i, where):
                d, h = where(i)
                if i >= 2:
                    act.wait_ge(square_added, 16 * n + i - 1)
                nc.scalar.activation(gbuf[:, i % 2], x_t[:, d, tokens(h)], ACT.Square).then_inc(squared, 1)

            def squares(n, where):
                for i in range(16):
                    square(n, i, where)

            def root(n, dst=rstd):
                for h in range(2):
                    act.wait_ge(mean_shifted, 2 * n + h + 1)
                    nc.scalar.activation(dst[:, tokens(h)], dst[:, tokens(h)], ACT.Sqrt).then_inc(root_ready, 1)

            def gate(c, f, func):
                for h in range(2):
                    act.wait_ge(gate_scaled, c * 4 + (2 * f + h + 1))
                    nc.scalar.activation(gbuf[:, h], gbuf[:, h], func).then_inc(gate_act, 1)

            def ffn_chunk(c):
                for f in range(2):
                    gate(c, f, ACT.Silu)
                    for h in range(2):
                        act.wait_ge(gated, c * 4 + (2 * f + h + 1))
                        nc.scalar.activation(f_hi[:, f, tokens(h)], hid[:, h], ACT.Copy).then_inc(f_rounded, 1)

            prep(0, half_major)
            squares(0, half_major)
            root(0)
            ffn_chunk(0)
            with act.Fori(1, CHUNKS) as c:
                ffn_chunk(c)
            prep(1, down_tile)
            squares(1, down_tile)
            root(1)

            act.wait_ge(x_stored, 16 * KT)
            act.dma_start(slopes[:, :], slopes_in).then_inc(slopes_loaded, 16)
            act.dma_start(dist[:, :], dists).then_inc(dist_loaded, 16)
            with act.Fori(CHUNKS, CHUNKS + 4) as c:
                for f in range(2):
                    gate(c, f, ACT.Sigmoid)

            def side_gate(n, tile, h):
                nc.scalar.activation(gbuf[:, h], gbuf[:, h], ACT.Sigmoid).then_inc(side_act, 1)
                act.wait_ge(side_act, n)
                act.dma_start(gates_kept[tile][:, tokens(h)], gbuf[:, h]).then_inc(side_stored[h], 16)

            def attend(b, m, p):
                g = m % GROUPS
                a4, a2, slot = b * 24 + 4 * m, b * 12 + 2 * m, b * 2 + m // GROUPS
                if p >= 2:
                    j = p - 2
                    act.wait_ge(o_ready, a4 + (j + 1))
                    if j == 0 and m > 0:
                        act.wait_ge(o_stored, b * 96 + 16 * m)
                    nc.scalar.activation(pair_in_natural(o_t[:, :], DILATION[g], j),
                                         pair_psum(ps[:, 6, 0:2 * P], DILATION[g]), ACT.Copy).then_inc(o_saved, 1)
                    if j == PAIRS - 1:
                        act.wait_ge(o_saved, a4 + PAIRS)
                        act.dma_start(o_kept[slot, g], o_t[:, :]).then_inc(o_stored, 16)
                if 1 <= p <= PAIRS:
                    j = p - 1
                    act.wait_ge(pt_turned, a4 + (j + 1))
                    nc.scalar.activation(pair_span(g, j, p_t[:, j % 2, :]), pair_span(g, j, ps[:, 5, :]),
                                         ACT.Copy).then_inc(pt_ready, 1)
                if p < 2:
                    act.wait_ge(v_turned, a2 + (p + 1))
                    nc.scalar.activation(v_tok[:, 4 * p:4 * p + 4, :],
                                         ps[:, 7, :].rearrange("p (b e) -> p b e", b=4), ACT.Copy).then_inc(v_ready, 1)
                if p < PAIRS:
                    act.wait_ge(max_negated, a4 + (p + 1))
                    for q in range(2):
                        blk = 2 * p + q
                        at = slice(q * 256 + (0 if has_prev(g, blk) else P), (q + 1) * 256)
                        last = nc.scalar.activation(s_buf[:, p % 2, at], s_buf[:, p % 2, at], ACT.Exp,
                                                    bias=neg_max[:, p % 2, q:q + 1], scale=SCALE,
                                                    accum_out=d_stat[:, slot, g, blk:blk + 1])
                    last.then_inc(p_ready, 1)

            with act.Fori(0, 2) as b:
                for hu in range(6, 2 * B_UNITS):
                    if hu >= 36:
                        i = hu - 36
                        act.wait_ge(proj_used, b * 44 + (hu + 1))
                        side_gate(b * 8 + (i + 1), b * 4 + i // 2, i % 2)
                    if hu < 42:
                        attend(b, hu // 6 - 1, hu % 6)
                act.wait_ge(o_stored, b * 96 + 96)

            def side(i):
                act.wait_ge(proj_used, 89 + i)
                side_gate(17 + i, KT + i // 2, i % 2)

            def rows(i):
                dst, dil = (m_rows, d_rows)[i // 3][0:SLOTS, i % 3, :], DILATION[i % 3]
                act.wait_ge(rows_turned, i + 1)
                for h in range(2):
                    src = ps[0:SLOTS, 4 + i % 2 * 2 + h, :]
                    if dil == 1:
                        view = dst[:, tokens(h)]
                    else:
                        view = dst.rearrange("p (i r) -> p r i", r=dil)[:, h * dil // 2:(h + 1) * dil // 2, :]
                        src = src.rearrange("p (r i) -> p r i", r=dil // 2)
                    last = nc.scalar.activation(view, src, ACT.Copy)
                last.then_inc(rows_ready, 1)

            def ysquare(i):
                d, h = tile_major(i)
                act.wait_ge(centred, i + 1)
                if i >= 2:
                    act.wait_ge(ysquare_added, i - 1)
                nc.scalar.activation(y_square[:, h], zbuf[:, d, tokens(h)], ACT.Square).then_inc(ysquared, 1)

            def ysquares(first, end):
                for i in range(first, end):
                    ysquare(i)

            def merge(n):
                s, h = tile_major(n)
                act.wait_ge(merged, n + 1)
                nc.scalar.activation(a_hi[:, s, tokens(h)], o_back(n)[:, 0], ACT.Copy).then_inc(a_rounded, 1)

            def load_o(n):
                s, h = tile_major(n)
                act.dma_start(o_back(n), o_kept[s].rearrange("g e t -> e g t")[:, :, tokens(h)])\
                   .then_inc(o_back_loaded[n % 4], 16)

            def load_factors(n):
                s, h = tile_major(n)
                act.dma_start(factor_back[:, n % 2],
                              factors_kept[s:s + 1, :, tokens(h)].to_broadcast([P, GROUPS, HALF]))\
                   .then_inc(factor_loaded[n % 2], 16)

            side(0)
            for h in range(2):
                act.wait_ge(ymean_ready, h + 1)
                nc.scalar.activation(y_mean[:, tokens(h)], bank(6 + h), ACT.Copy).then_inc(mean_saved, 1)
            rows(0)
            side(1)
            rows(1)
            rows(2)
            ysquares(0, 2)
            rows(3)
            rows(4)
            rows(5)
            side(2)
            ysquares(2, 3)
            for g in range(GROUPS):
                act.wait_ge(row_step, 3 + g)
                nc.scalar.activation(m_rows[0:SLOTS, g, :], m_rows[0:SLOTS, g, :], ACT.Exp,
                                     scale=SCALE).then_inc(exp_ready, 1)
            side(3)
            ysquares(3, 4)
            act.wait_ge(o_stored, 16 * SLOTS * GROUPS)
            load_o(0)
            load_o(1)
            side(4)
            ysquares(4, 6)
            act.wait_ge(weights_ready, 3)
            act.dma_start(factors_kept, m_rows[0:SLOTS, :, :]).then_inc(factors_stored, 16)
            side(5)
            act.wait_ge(factors_stored, 16)
            load_factors(0)
            load_factors(1)
            load_o(2)
            load_o(3)
            ysquares(6, 7)
            side(6)
            ysquares(7, 8)
            side(7)
            ysquares_until = (9, 11, 12, 13, 15, 16, 16, 16)
            for n in range(8):
                merge(n)
                side(8 + n)
                if n + 2 < 8:
                    act.wait_ge(a_ready, n + 1)
                    load_factors(n + 2)
                if 2 <= n < 6:
                    load_o(n + 2)
                ysquares(ysquares_until[n - 1] if n else 8, ysquares_until[n])
            for h in range(2):
                act.wait_ge(mean_shifted, 4 + h + 1)
                nc.scalar.activation(acc[:, tokens(h)], acc[:, tokens(h)], ACT.Sqrt).then_inc(root_ready, 1)

            def load_gate(n):
                if n >= 2:
                    act.wait_ge(ya_used if n < 18 else yc_gated, n - 1 if n < 18 else n - 17)
                tile, h = tile_major(n)
                act.dma_start(gbuf[:, n % 2], gates_kept[(tile + KT) % (2 * KT)][:, tokens(h)])\
                   .then_inc(gate_back[n % 2], 16)

            for h in range(2):
                act.wait_ge(side_stored[h], 16 * 16)
            load_gate(0)
            load_gate(1)
            for i in range(16):
                d, h = tile_major(i)
                act.wait_ge(norm_made, i + 1)
                nc.scalar.activation(hid[:, i % 2], hid[:, i % 2], ACT.Silu,
                                     bias=vec[:, V_LNB + d:V_LNB + d + 1]).then_inc(norm_act, 1)
                act.wait_ge(norm_act, i + 1)
                nc.scalar.activation(h_hi[:, d, tokens(h)], hid[:, i % 2], ACT.Copy).then_inc(norm_rounded, 1)
                if i >= 1:
                    load_gate(i + 1)
            load_gate(17)

            for i in range(16):
                d, h = tile_major(i)
                act.wait_ge(mixed_made, i + 1)
                nc.scalar.activation(mx_hi[:, d, tokens(h)], hid[:, i % 2], ACT.Copy).then_inc(mx_rounded, 1)
                if i + 2 < 16:
                    load_gate(18 + i)

            act.wait_ge(mixed_made, 16)
            for d in range(KT):
                act.dma_start(x_t[:, d], x_kept[d]).then_inc(x_back[d], 16)
            prep(2, tile_major, squares=True)
            root(3)

            ffn_chunk(CHUNKS + 4)
            with act.Fori(CHUNKS + 5, 2 * CHUNKS + 4) as c:
                ffn_chunk(c)
            for i in range(16):
                act.wait_ge(down_added, 16 * (2 * CHUNKS - 1) + i + 1)
                square(3, i, down_tile)
            act.wait_ge(mean_shifted, 9)
            nc.scalar.activation(tok_rstd[:, :], tok_rstd[:, :], ACT.Sqrt).then_inc(root_ready, 1)

        @block.vector
        def _(dve):
            v = nc.vector

            def prep_scale(n, i, gain, where):
                d, h = where(i)
                if i >= 2:
                    dve.wait_ge(prep_ready, 16 * n + i - 1)
                v.tensor_scalar(hid[:, i % 2], x_t[:, d, tokens(h)], vec[:, gain + d:gain + d + 1], None,
                                ALU.mult).then_inc(prep_scaled, 1)

            def prep_rest(n, i, where):
                d, h = where(i)
                dve.wait_ge(prep_rounded, 16 * n + i + 1)
                v.tensor_tensor(h_lo[:, d, tokens(h)], hid[:, i % 2], h_hi[:, d, tokens(h)].bitcast(F32),
                                ALU.subtract).then_inc(prep_ready, 1)

            def add_square(n, i, where):
                d, h = where(i)
                dve.wait_ge(squared, 16 * n + i + 1)
                if d == 0:
                    v.tensor_copy(acc[:, tokens(h)], gbuf[:, i % 2]).then_inc(square_added, 1)
                else:
                    before = max(k for k in range(i) if where(k)[1] == h)
                    dve.wait_ge(square_added, 16 * n + before + 1)
                    v.tensor_tensor(acc[:, tokens(h)], acc[:, tokens(h)], gbuf[:, i % 2],
                                    ALU.add).then_inc(square_added, 1)

            def inverse_root(n, m, dst=rstd):
                for h in range(2):
                    dve.wait_ge(mean_ready, 2 * n + h + 1)
                    v.tensor_scalar(dst[:, tokens(h)], bank(6 + h), EPS, None, ALU.add).then_inc(mean_shifted, 1)
                for h in range(2):
                    dve.wait_ge(root_ready, m + h + 1)
                    v.reciprocal(dst[:, tokens(h)], dst[:, tokens(h)]).then_inc(rstd_ready, 1)
                dve.wait_ge(rstd_ready, 2 * n + 2)

            def gate(c, f, first=False):
                for h in range(2):
                    dve.wait_ge(gate_ready, c * 4 + (2 * f + h + 1))
                    if f == 1 or not first:
                        dve.wait_ge(gated, c * 4 + (2 * f + h - 1))
                    v.tensor_tensor(gbuf[:, h], bank(4 * f + h), rstd[:, tokens(h)], ALU.mult)\
                     .then_inc(gate_scaled, 1)
                    dve.wait_ge(gate_act, c * 4 + (2 * f + h + 1))
                    v.tensor_tensor(gbuf[:, h], gbuf[:, h], rstd[:, tokens(h)], ALU.mult)\
                     .then_inc(gate_weighted, 1)

            def up(c, f, h, dst):
                dve.wait_ge(up_ready, c * 4 + (2 * f + h + 1))
                dve.wait_ge(gate_weighted, c * 4 + (2 * f + h + 1))
                v.tensor_tensor(dst, bank(4 * f + 2 + h), gbuf[:, h], ALU.mult).then_inc(gated, 1)

            def ffn_gates(c, cf, first=False):
                for f in range(2):
                    gate(c, f, first)
                    for h in range(2):
                        if f == 1:
                            dve.wait_ge(f_ready, cf * 4 + (h + 1))
                        up(c, f, h, hid[:, h])
                        dve.wait_ge(f_rounded, cf * 4 + (2 * f + h + 1))
                        v.tensor_tensor(f_lo[:, f, tokens(h)], hid[:, h], f_hi[:, f, tokens(h)].bitcast(F32),
                                        ALU.subtract).then_inc(f_ready, 1)

            def add_down(cd, i):
                d, h = down_tile(i)
                dve.wait_ge(down_ready, cd * 16 + (i + 1))
                v.scalar_tensor_tensor(x_t[:, d, tokens(h)], bank(i % 8), 0.5, x_t[:, d, tokens(h)],
                                       ALU.mult, ALU.add).then_inc(down_added, 1)

            dve.wait_ge(vec_loaded, 16)
            for i in range(17):
                if i < 16:
                    d, h = half_major(i)
                    dve.wait_ge(x_loaded[d][h], 16)
                    prep_scale(0, i, V_NORM1, half_major)
                if i >= 1:
                    prep_rest(0, i - 1, half_major)
            for i in range(16):
                add_square(0, i, half_major)
            inverse_root(0, 0)
            ffn_gates(0, 0, first=True)
            for i in range(16):
                add_down(0, i)
            with dve.Fori(1, CHUNKS - 1) as c:
                ffn_gates(c, c)
                for i in range(16):
                    add_down(c, i)
            ffn_gates(CHUNKS - 1, CHUNKS - 1)
            for i in range(17):
                if i < 16:
                    add_down(CHUNKS - 1, i)
                    dve.wait_ge(down_added, 16 * (CHUNKS - 1) + i + 1)
                    prep_scale(1, i, V_MIX, down_tile)
                if i >= 1:
                    prep_rest(1, i - 1, down_tile)
            for i in range(16):
                add_square(1, i, down_tile)
            inverse_root(1, 2)

            dve.wait_ge(x_stored, 16 * KT)
            v.memset(zbuf[:, :, 0:PAD], 0.0).then_inc(conv_step, 1)
            v.memset(acc[:, :], 0.0).then_inc(ysum_added, 1)

            def conv_taps(tile, first, end):
                y = zbuf[:, tile, 0:SEQ]
                for t in range(first, end):
                    z = zbuf[:, tile + 1, t:t + SEQ]
                    k = vec[:, bass.ds(tile * TAPS + (V_TAPS + t), 1)]
                    if t == 0:
                        dve.wait_ge(conv_step, tile * TAPS + 1)
                        v.tensor_scalar(y, z, k, vec[:, bass.ds(tile + V_DWB, 1)], ALU.mult, ALU.add)\
                         .then_inc(conv_step, 1)
                    else:
                        dve.wait_ge(conv_step, tile * TAPS + (t + 1))
                        v.scalar_tensor_tensor(y, z, k, y, ALU.mult, ALU.add).then_inc(conv_step, 1)
                if end == TAPS:
                    dve.wait_ge(conv_step, tile * TAPS + (TAPS + 1))
                    dve.wait_ge(ysum_added, tile + 1)
                    v.tensor_tensor(acc[:, :], acc[:, :], y, ALU.add).then_inc(ysum_added, 1)

            with dve.Fori(0, 2) as j:
                for q in range(4):
                    c = j * 2 + (CHUNKS + q // 2)
                    if q == 1:
                        dve.wait_ge(gated, j * 2 + (4 * CHUNKS + 2))
                    gate(c, q % 2)
                    if q > 0:
                        conv_taps(j, TAPS * (q - 1) // 3, TAPS * (2 * q - 1) // 6)
                    for h in range(2):
                        up(c, q % 2, h, zbuf[:, j * 4 + (q + 1), PAD + h * HALF:PAD + (h + 1) * HALF])
                        if q > 0 and h == 0:
                            conv_taps(j, TAPS * (2 * q - 1) // 6, TAPS * q // 3)

            def take_proj(b, u, h):
                m, kind = u // 3, u % 3
                dil = DILATION[m % GROUPS]
                dst = (q_t[:, m % 2, :], k_t[:, m % 2, :], v_t[:, :])[kind]
                dve.wait_ge(proj_ready, b * 44 + (2 * u + h + 1))
                v.tensor_tensor(split_permuted(dst, dil, h), split_natural(bank((2 * u + h) % 4), dil, h),
                                split_natural(rstd[:, tokens(h)], dil, h), ALU.mult).then_inc(proj_used, 1)

            def take_gate(b, u, h, n, src):
                dve.wait_ge(proj_ready, b * 44 + (2 * u + h + 1))
                if n is not None:
                    dve.wait_ge(side_stored[h], n)
                v.tensor_tensor(gbuf[:, h], src, rstd[:, tokens(h)], ALU.mult).then_inc(proj_used, 1)

            def soften(b, m, p):
                g = m % GROUPS
                a4, slot = b * 24 + 4 * m, b * 2 + m // GROUPS
                dst = s_buf[:, p % 2, :]
                d = dist_diag if g == 2 else (dist_full if has_prev(g, 2 * p) else dist_full[:, P:512])
                dve.wait_ge(scores_ready, a4 + (p + 1))
                v.scalar_tensor_tensor(pair_span(g, p, dst), d, slopes[:, bass.ds(slot * GROUPS + g, 1)],
                                       pair_span(g, p, ps[:, 4, :]), ALU.mult, ALU.add).then_inc(s_made, 1)
                dve.wait_ge(s_made, a4 + (p + 1))
                peaks = m_stat[:, slot, g, 2 * p:2 * p + 2]
                if g == 2 or has_prev(g, 2 * p):
                    s = dst.rearrange("p (a k) -> p a k", a=2)
                    v.tensor_reduce(peaks, s[:, :, P:256] if g == 2 else s, AXX, ALU.max).then_inc(max_made, 2)
                else:
                    v.tensor_reduce(peaks[:, 0:1], dst[:, P:256], AXX, ALU.max).then_inc(max_made, 1)
                    v.tensor_reduce(peaks[:, 1:2], dst[:, 256:512], AXX, ALU.max).then_inc(max_made, 1)
                dve.wait_ge(max_made, a4 * 2 + (2 * p + 2))
                v.tensor_scalar(neg_max[:, p % 2, :], peaks, -SCALE, None, ALU.mult).then_inc(max_negated, 1)

            dve.wait_ge(slopes_loaded, 16)
            dve.wait_ge(dist_loaded, 16)
            with dve.Fori(0, 2) as b:
                for hu in range(2 * B_UNITS):
                    u, h = tile_major(hu)
                    if u < 18:
                        take_proj(b, u, h)
                    else:
                        take_gate(b, u, h, b * 64 + 16 * (u - 18) if u > 18 else None, bank(hu % 4))
                    if 6 <= hu < 42 and hu % 6 < PAIRS:
                        soften(b, hu // 6 - 1, hu % 6)
                    if hu == 0:
                        dve.wait_ge(gated, 4 * (CHUNKS + 4))
                    i = hu % 14
                    if hu < 42:
                        conv_taps(b * 3 + (2 + hu // 14), TAPS * i // 14, TAPS * (i + 1) // 14)
                for h in range(2):
                    dve.wait_ge(side_stored[h], b * 64 + 64)

            def side(i):
                take_gate(2, i // 2, i % 2, 128 + 16 * (i // 2), bank(i % 6))

            side(0)
            side(1)
            top = hid[0:SLOTS, :, :].rearrange("p a t -> p (a t)")
            m_g = [m_rows[0:SLOTS, g, :] for g in range(GROUPS)]
            d_g = [d_rows[0:SLOTS, g, :] for g in range(GROUPS)]
            dve.wait_ge(rows_ready, 3)
            v.tensor_tensor(top, m_g[0], m_g[1], ALU.max).then_inc(row_step, 1)
            dve.wait_ge(row_step, 1)
            v.tensor_tensor(top, top, m_g[2], ALU.max).then_inc(row_step, 1)
            dve.wait_ge(row_step, 2)
            for g in range(GROUPS):
                v.tensor_tensor(m_g[g], m_g[g], top, ALU.subtract).then_inc(row_step, 1)
            side(2)
            dve.wait_ge(rows_ready, 6)
            for g in range(GROUPS):
                dve.wait_ge(exp_ready, g + 1)
                v.tensor_tensor(d_g[g], d_g[g], m_g[g], ALU.mult).then_inc(row_step, 1)
            side(3)
            side(4)
            dve.wait_ge(row_step, 7)
            v.tensor_tensor(d_g[0], d_g[0], d_g[1], ALU.add).then_inc(row_step, 1)
            dve.wait_ge(row_step, 9)
            v.tensor_tensor(d_g[0], d_g[0], d_g[2], ALU.add).then_inc(row_step, 1)
            dve.wait_ge(row_step, 10)
            v.reciprocal(d_g[0], d_g[0]).then_inc(row_step, 1)
            dve.wait_ge(row_step, 11)
            for g in range(GROUPS):
                v.tensor_tensor(m_g[g], m_g[g], d_g[0], ALU.mult).then_inc(weights_ready, 1)
            for i in range(5, 8):
                side(i)

            def merge(n):
                s, h = tile_major(n)
                o = [o_back(n)[:, g] for g in range(GROUPS)]
                dve.wait_ge(o_back_loaded[n % 4], 16 * (n // 4 + 1))
                dve.wait_ge(factor_loaded[n % 2], 16 * (n // 2 + 1))
                for g in range(GROUPS):
                    v.tensor_tensor(o[g], o[g], factor_back[:, n % 2, g], ALU.mult).then_inc(factor_used, 1)
                dve.wait_ge(factor_used, GROUPS * n + 2)
                v.tensor_tensor(o[0], o[0], o[1], ALU.add).then_inc(merge_step, 1)
                dve.wait_ge(merge_step, n + 1)
                dve.wait_ge(factor_used, GROUPS * n + 3)
                v.tensor_tensor(o[0], o[0], o[2], ALU.add).then_inc(merged, 1)
                dve.wait_ge(a_rounded, n + 1)
                v.tensor_tensor(a_lo[:, s, tokens(h)], o[0], a_hi[:, s, tokens(h)].bitcast(F32),
                                ALU.subtract).then_inc(a_ready, 1)

            for n in range(8):
                merge(n)
                side(8 + n)
                if n == 6:
                    for h in range(2):
                        dve.wait_ge(mean_ready, 4 + h + 1)
                        v.tensor_scalar(acc[:, tokens(h)], bank(6 + h), EPS, None, ALU.add).then_inc(mean_shifted, 1)
            for h in range(2):
                dve.wait_ge(root_ready, 4 + h + 1)
                v.reciprocal(acc[:, tokens(h)], acc[:, tokens(h)]).then_inc(rstd_ready, 1)

            dve.wait_ge(rstd_ready, 6)
            for i in range(17):
                if i < 16:
                    d, h = tile_major(i)
                    if i >= 2:
                        dve.wait_ge(norm_ready, i - 1)
                    v.scalar_tensor_tensor(hid[:, i % 2], zbuf[:, d, tokens(h)], vec[:, V_LNG + d:V_LNG + d + 1],
                                           acc[:, tokens(h)], ALU.mult, ALU.mult).then_inc(norm_made, 1)
                if i >= 1:
                    d, h = tile_major(i - 1)
                    dve.wait_ge(norm_rounded, i)
                    v.tensor_tensor(h_lo[:, d, tokens(h)], hid[:, (i - 1) % 2], h_hi[:, d, tokens(h)].bitcast(F32),
                                    ALU.subtract).then_inc(norm_ready, 1)
                    dve.wait_ge(ya_ready, i)
                    dve.wait_ge(gate_back[(i - 1) % 2], 16 * ((i - 1) // 2 + 1))
                    v.tensor_tensor(zbuf[:, d, tokens(h)], projection_bank(i - 1), gbuf[:, (i - 1) % 2],
                                    ALU.mult).then_inc(ya_used, 1)

            for i in range(17):
                if i < 16:
                    d, h = tile_major(i)
                    dve.wait_ge(yc_ready, i + 1)
                    dve.wait_ge(gate_back[i % 2], 16 * (8 + i // 2 + 1))
                    dve.wait_ge(mx_ready if i >= 2 else norm_ready, i - 1 if i >= 2 else 16)
                    v.tensor_tensor(hid[:, i % 2], projection_bank(i), gbuf[:, i % 2], ALU.mult).then_inc(yc_gated, 1)
                    dve.wait_ge(yc_gated, i + 1)
                    dve.wait_ge(ya_used, i + 1)
                    v.tensor_tensor(hid[:, i % 2], hid[:, i % 2], zbuf[:, d, tokens(h)], ALU.add)\
                     .then_inc(mixed_made, 1)
                if i >= 1:
                    d, h = tile_major(i - 1)
                    dve.wait_ge(mx_rounded, i)
                    v.tensor_tensor(mx_lo[:, d, tokens(h)], hid[:, (i - 1) % 2], mx_hi[:, d, tokens(h)].bitcast(F32),
                                    ALU.subtract).then_inc(mx_ready, 1)

            for i in range(17):
                if i < 16:
                    d, h = tile_major(i)
                    dve.wait_ge(wo_ready, i + 1)
                    dve.wait_ge(x_back[d], 16)
                    v.tensor_tensor(x_t[:, d, tokens(h)], bank(i % 8), x_t[:, d, tokens(h)], ALU.add)\
                     .then_inc(wo_added, 1)
                    dve.wait_ge(wo_added, i + 1)
                    prep_scale(2, i, V_NORM2, tile_major)
                if i >= 1:
                    prep_rest(2, i - 1, tile_major)
                    add_square(2, i - 1, tile_major)
            inverse_root(3, 6)

            ffn_gates(CHUNKS + 4, CHUNKS)
            for i in range(16):
                add_down(CHUNKS, i)
            with dve.Fori(CHUNKS + 1, 2 * CHUNKS - 1) as c:
                ffn_gates(c + 4, c)
                for i in range(16):
                    add_down(c, i)
            ffn_gates(2 * CHUNKS + 3, 2 * CHUNKS - 1)
            for i in range(17):
                if i < 16:
                    add_down(2 * CHUNKS - 1, i)
                if i >= 1:
                    add_square(3, i - 1, down_tile)
            dve.wait_ge(mean_ready, 9)
            v.tensor_scalar(tok_rstd[:, :], ps[:, 6, 0:NBLK], EPS, None, ALU.add).then_inc(mean_shifted, 1)
            dve.wait_ge(root_ready, 9)
            v.reciprocal(tok_rstd[:, :], tok_rstd[:, :]).then_inc(rstd_ready, 1)
            for i in range(16):
                d, h = half_major(i)
                dve.wait_ge(rstd_spread, h + 1)
                v.scalar_tensor_tensor(x_t[:, d, tokens(h)], x_t[:, d, tokens(h)], vec[:, V_FINAL + d:V_FINAL + d + 1],
                                       bank(h), ALU.mult, ALU.mult).then_inc(final_made, 1)


def _shape_constants():
    consts = np.zeros((P, N_CONST), np.float32)
    consts[:, C_IDENT:C_IDENT + P] = np.eye(P)
    consts[:, C_MEAN:C_MEAN + P] = 1.0 / D_MODEL
    slope_cols = np.zeros((P, N_SLOPES), np.float32)
    heads = np.arange(1, SLOTS * GROUPS + 1, dtype=np.float32)
    slopes = np.power(np.float32(2.0), -8.0 * heads / np.float32(SLOTS * GROUPS))
    for s in range(SLOTS):
        for g in range(GROUPS):
            slope_cols[:, s * GROUPS + g] = -slopes[g * SLOTS + s] * DILATION[g] / SCALE
    q, k = np.arange(P)[:, None], np.arange(2 * P)[None, :]
    steps = P + q - k
    full = np.where((steps >= 0) & (steps <= P), steps, MASKED)
    k = np.arange(P)[None, :]
    own = P // 2
    diag = np.where((q // own == k // own) & (q >= k), q - k, MASKED)
    dists = np.concatenate([full, full, diag, diag], axis=1).astype(np.float32)
    return consts, slope_cols, dists


def _columns(w, first):
    return w[:, first:first + P].reshape(KT, P, P).transpose(1, 0, 2).reshape(P, 1024)


def _ffn_slabs(gate, up, down):
    for c in range(CHUNKS):
        for f in range(2):
            yield _columns(gate, (2 * c + f) * P)
            yield _columns(up, (2 * c + f) * P)
        rows = down[2 * c * P:2 * (c + 1) * P].reshape(2, P, 2, HALF)
        for j in range(2):
            yield rows[:, :, j].transpose(1, 0, 2).reshape(P, 1024)


def _slabs(t):
    w_in = t["w_in"][0]
    q0 = 2 * D_MODEL
    width = SLOTS * GROUPS * P
    gates0 = q0 + 3 * width
    yield from _ffn_slabs(t["ffn1_w_gate"][0], t["ffn1_w_up"][0], t["ffn1_w_down"][0])
    for i in range(KT):
        yield _columns(w_in, D_MODEL + i * P)
        yield _columns(w_in, i * P)
    for b in range(2):
        for s in (2 * b, 2 * b + 1):
            for g in range(GROUPS):
                for kind in range(3):
                    yield _columns(w_in, q0 + kind * width + (g * SLOTS + s) * P)
        for i in range(4):
            yield _columns(w_in, gates0 + (4 * b + i) * P)
    for i in range(KT):
        yield _columns(w_in, gates0 + D_MODEL + i * P)
    rows = t["attn_w_out"][0].reshape(SLOTS, P, 4, 256)
    for j in range(4):
        yield rows[:, :, j].transpose(1, 0, 2).reshape(P, 1024)
    for i in range(KT):
        yield _columns(t["conv_w_out"][0], i * P)
    for i in range(KT):
        yield _columns(t["w_o"][0], i * P)
    yield from _ffn_slabs(t["ffn2_w_gate"][0], t["ffn2_w_up"][0], t["ffn2_w_down"][0])


def kernel(**inputs):
    import concourse.bacc as _bacc
    from concourse.bass_utils import run_bass_kernel_spmd as _run

    t = {name: np.asarray(a) for name, a in inputs.items()}
    feature_cols = [t[n].reshape(KT, P).T for n in
                    ("ffn1_norm", "mix_norm", "ffn2_norm", "final_norm", "conv_ln_gain", "conv_ln_bias",
                     "conv_dw_bias")]
    taps = t["conv_dw_kernel"][0].reshape(TAPS, KT, P).transpose(2, 1, 0).reshape(P, KT * TAPS)
    consts, slope_cols, dists = _shape_constants()
    arrays = {
        "w_slabs": np.stack(list(_slabs(t))),
        "x_in": np.ascontiguousarray(t["x"][0].T).reshape(KT, P, SEQ),
        "vecs": np.ascontiguousarray(np.concatenate(feature_cols + [taps], axis=1)),
        "consts": consts,
        "slopes_in": slope_cols,
        "dists": dists,
    }
    nc = _bacc.Bacc("TRN2", target_bir_lowering=False, num_devices=1)
    args = [nc.dram_tensor(n, a.shape, F32, kind="ExternalInput").ap() for n, a in arrays.items()]
    out = nc.dram_tensor("out_t", (KT, P, SEQ), F32, kind="ExternalOutput").ap()
    build_block(nc, *args, out)
    r = _run(nc, [arrays], core_ids=[0])
    return np.ascontiguousarray(r.results[0]["out_t"].reshape(1, D_MODEL, SEQ).transpose(0, 2, 1))
```
